# Optimizing a Trainium2 kernel written in Bass

```python
import math
import jax, jax.numpy as jnp
from jax import lax
import numpy as np

D_MODEL = 1024
BATCH = 1
SEQ = 256
DEPTH = 1

C_CONV = D_MODEL
K_CONV = 31
HEAD_DIM = 64
N_HEADS = D_MODEL // HEAD_DIM
N_KV_HEADS = N_HEADS // 8
GROUP = N_HEADS // N_KV_HEADS
WINDOW = 128
Q_BLOCK = 128
N_EXPERTS = 32
TOP_K = 4
D_FF = D_MODEL
SWIGLU_LIMIT = 7.0
SWIGLU_ALPHA = 1.702
MOE_BLOCK = 128
EPS = 1e-5

N_GLU = 2 * C_CONV
N_Q = N_HEADS * HEAD_DIM
N_KV = N_KV_HEADS * HEAD_DIM
N_GATE = 2 * D_MODEL
N_IN = N_GLU + N_Q + 2 * N_KV + N_GATE

kernel_name = "hybrid_conformer_swa_sink_alibi_moe"

def rms_norm(x, g):
    xf = x.astype(jnp.float32)
    y = xf * lax.rsqrt(jnp.mean(xf * xf, axis=-1, keepdims=True) + EPS)
    return (y * g.astype(jnp.float32)).astype(x.dtype)

def layer_norm(x, g, b):
    xf = x.astype(jnp.float32)
    mu = jnp.mean(xf, axis=-1, keepdims=True)
    var = jnp.mean(jnp.square(xf - mu), axis=-1, keepdims=True)
    y = (xf - mu) * lax.rsqrt(var + EPS)
    return (y * g.astype(jnp.float32) + b.astype(jnp.float32)).astype(x.dtype)

def alibi_slopes(n_heads):
    return jnp.asarray([2.0 ** (-8.0 * (i + 1) / n_heads) for i in range(n_heads)], dtype=jnp.float32)

def conformer_conv(a, b, conv_w, conv_b, ln_g, ln_b, w_o, b_o):
    u = a * jax.nn.sigmoid(b)
    u = lax.conv_general_dilated(
        u, conv_w[:, None, :].astype(u.dtype), window_strides=(1,),
        padding=[(K_CONV - 1, 0)], dimension_numbers=("NWC", "WIO", "NWC"),
        feature_group_count=C_CONV) + conv_b
    u = jax.nn.silu(layer_norm(u, ln_g, ln_b))
    return u @ w_o + b_o

def sliding_window_attention(q, k, v, sinks):
    B, T = q.shape[0], q.shape[1]
    nb = T // Q_BLOCK
    qb = q.reshape(B, nb, Q_BLOCK, N_KV_HEADS, GROUP, HEAD_DIM)

    def band(t):
        cur = t.reshape(B, nb, Q_BLOCK, N_KV_HEADS, HEAD_DIM)
        prev = jnp.pad(t, ((0, 0), (Q_BLOCK, 0), (0, 0), (0, 0)))[:, :T]
        prev = prev.reshape(B, nb, Q_BLOCK, N_KV_HEADS, HEAD_DIM)
        return jnp.concatenate([prev, cur], axis=2)

    kb, vb = band(k), band(v)
    scale = 1.0 / math.sqrt(HEAD_DIM)
    s = jnp.einsum("bnqkgd,bnskd->bnkgqs", qb, kb).astype(jnp.float32) * scale

    qi = jnp.arange(Q_BLOCK)[:, None]
    sj = jnp.arange(2 * Q_BLOCK)[None, :]
    dist = (qi + Q_BLOCK - sj).astype(jnp.float32)
    key_pos = jnp.arange(nb)[:, None] * Q_BLOCK - Q_BLOCK + jnp.arange(2 * Q_BLOCK)[None, :]
    valid = ((dist >= 0) & (dist < WINDOW))[None] & (key_pos >= 0)[:, None, :]

    slopes = alibi_slopes(N_HEADS).reshape(N_KV_HEADS, GROUP)
    s = s - slopes[:, :, None, None] * dist
    s = jnp.where(valid[None, :, None, None], s, -jnp.inf)

    sink = sinks.astype(jnp.float32).reshape(N_KV_HEADS, GROUP)[None, None, :, :, None, None]
    m = jnp.maximum(jnp.max(s, axis=-1, keepdims=True), sink)
    p = jnp.exp(s - m)
    p = p / (jnp.sum(p, axis=-1, keepdims=True) + jnp.exp(sink - m))
    o = jnp.einsum("bnkgqs,bnskd->bnqkgd", p.astype(v.dtype), vb)
    return o.reshape(B, T, N_HEADS * HEAD_DIM)

def moe_ffn(h, w_router, b_router, w_gate, b_gate, w_up, b_up, w_down, b_down):
    B, T, D = h.shape
    N = B * T
    hf = h.reshape(N, D)
    logits = (hf @ w_router + b_router).astype(jnp.float32)
    top_v, top_e = lax.top_k(logits, TOP_K)
    top_w = jax.nn.softmax(top_v, axis=-1)

    A = N * TOP_K
    flat_e = top_e.reshape(A)
    flat_tok = jnp.repeat(jnp.arange(N, dtype=jnp.int32), TOP_K)
    flat_w = top_w.reshape(A)
    order = jnp.argsort(flat_e, stable=True)
    sorted_e = flat_e[order]
    counts = jnp.bincount(flat_e, length=N_EXPERTS)
    padded = ((counts + MOE_BLOCK - 1) // MOE_BLOCK) * MOE_BLOCK
    pad_end = jnp.cumsum(padded)
    pad_start = pad_end - padded
    start = jnp.cumsum(counts) - counts
    dest = pad_start[sorted_e] + jnp.arange(A) - start[sorted_e]

    n_blocks = (A + N_EXPERTS * (MOE_BLOCK - 1) + MOE_BLOCK - 1) // MOE_BLOCK
    P = n_blocks * MOE_BLOCK
    row_tok = jnp.zeros((P,), jnp.int32).at[dest].set(flat_tok[order])
    row_w = jnp.zeros((P,), jnp.float32).at[dest].set(flat_w[order])
    block_start = jnp.arange(n_blocks) * MOE_BLOCK
    block_e = jnp.minimum(jnp.sum(block_start[:, None] >= pad_end[None, :], axis=1), N_EXPERTS - 1)
    xb = hf[row_tok].reshape(n_blocks, MOE_BLOCK, D)

    def expert_block(args):
        xblk, e = args
        g = xblk @ w_gate[e] + b_gate[e]
        u = xblk @ w_up[e] + b_up[e]
        g = jnp.minimum(g, SWIGLU_LIMIT)
        u = jnp.clip(u, -SWIGLU_LIMIT, SWIGLU_LIMIT)
        a = (u + 1.0) * (g * jax.nn.sigmoid(SWIGLU_ALPHA * g))
        return a @ w_down[e] + b_down[e]

    yb = lax.map(expert_block, (xb, block_e)).reshape(P, D)
    y = jnp.zeros((N, D), jnp.float32).at[row_tok].add(yb.astype(jnp.float32) * row_w[:, None])
    return y.astype(h.dtype).reshape(B, T, D)

def setup_inputs(seed: int = 0) -> dict:
    key = jax.random.key(seed)
    ks = jax.random.split(key, 26)
    f = jnp.float32
    nrm = lambda k, shape, s: jax.random.normal(k, shape, f) * s
    D, F, E = D_MODEL, D_FF, N_EXPERTS
    return {
        "x": nrm(ks[0], (BATCH, SEQ, D), 1.0),
        "g_mix": 1.0 + nrm(ks[1], (D,), 0.05),
        "w_in": nrm(ks[2], (D, N_IN), D ** -0.5),
        "b_in": nrm(ks[3], (N_IN,), 0.02),
        "conv_w": nrm(ks[4], (K_CONV, C_CONV), K_CONV ** -0.5),
        "conv_b": nrm(ks[5], (C_CONV,), 0.02),
        "conv_ln_g": 1.0 + nrm(ks[6], (C_CONV,), 0.05),
        "conv_ln_b": nrm(ks[7], (C_CONV,), 0.02),
        "w_conv_out": nrm(ks[8], (C_CONV, D), C_CONV ** -0.5),
        "b_conv_out": nrm(ks[9], (D,), 0.02),
        "attn_sinks": nrm(ks[10], (N_HEADS,), 0.5),
        "w_attn_out": nrm(ks[11], (N_Q, D), N_Q ** -0.5),
        "b_attn_out": nrm(ks[12], (D,), 0.02),
        "w_out": nrm(ks[13], (D, D), D ** -0.5),
        "g_ffn": 1.0 + nrm(ks[14], (D,), 0.05),
        "w_router": nrm(ks[15], (D, E), D ** -0.5),
        "b_router": nrm(ks[16], (E,), 0.01),
        "w_gate": nrm(ks[17], (E, D, F), D ** -0.5),
        "b_gate": nrm(ks[18], (E, F), 0.02),
        "w_up": nrm(ks[19], (E, D, F), D ** -0.5),
        "b_up": nrm(ks[20], (E, F), 0.02),
        "w_down": nrm(ks[21], (E, F, D), F ** -0.5),
        "b_down": nrm(ks[22], (E, D), 0.02),
        "g_final": 1.0 + nrm(ks[23], (D,), 0.05),
    }

def reference(x, g_mix, w_in, b_in, conv_w, conv_b, conv_ln_g, conv_ln_b, w_conv_out,
              b_conv_out, attn_sinks, w_attn_out, b_attn_out, w_out, g_ffn, w_router,
              b_router, w_gate, b_gate, w_up, b_up, w_down, b_down, g_final):
    B, T, D = x.shape
    for _ in range(DEPTH):
        h = rms_norm(x, g_mix)
        z = h @ w_in + b_in
        o0 = 0
        glu_a = z[..., o0:o0 + C_CONV]; o0 += C_CONV
        glu_b = z[..., o0:o0 + C_CONV]; o0 += C_CONV
        q = z[..., o0:o0 + N_Q].reshape(B, T, N_HEADS, HEAD_DIM); o0 += N_Q
        k = z[..., o0:o0 + N_KV].reshape(B, T, N_KV_HEADS, HEAD_DIM); o0 += N_KV
        v = z[..., o0:o0 + N_KV].reshape(B, T, N_KV_HEADS, HEAD_DIM); o0 += N_KV
        gate_conv = jax.nn.sigmoid(z[..., o0:o0 + D]); o0 += D
        gate_attn = jax.nn.sigmoid(z[..., o0:o0 + D])

        y_conv = conformer_conv(glu_a, glu_b, conv_w, conv_b, conv_ln_g, conv_ln_b,
                                w_conv_out, b_conv_out)
        y_attn = sliding_window_attention(q, k, v, attn_sinks) @ w_attn_out + b_attn_out
        x = x + (gate_conv * y_conv + gate_attn * y_attn) @ w_out

        x = x + moe_ffn(rms_norm(x, g_ffn), w_router, b_router, w_gate, b_gate,
                        w_up, b_up, w_down, b_down)
    return rms_norm(x, g_final)


_drawn_inputs = setup_inputs


def setup_inputs(seed=0):
    import zlib

    import numpy as np

    out = dict(_drawn_inputs(seed))
    spreads = {}
    factors = {'conv_ln_b': 3.074, 'b_gate': 6.501, 'b_up': 8.0, 'b_down': 6.139}
    for name, (base, spread) in spreads.items():
        noise = np.random.default_rng([zlib.crc32(name.encode()), seed]).standard_normal(out[name].shape)
        drawn = base * np.exp(spread * noise) if base else spread * noise
        out[name] = __import__('jax').numpy.asarray(drawn.astype(out[name].dtype))
    for name, factor in factors.items():
        out[name] = (out[name] * factor).astype(out[name].dtype)
    return out
```

```python
import concourse.bass as bass
from concourse import mybir
from contextlib import ExitStack

P = 128
D = 1024
T = 256
TT = T // P
C = D // P
KTAPS = 31
HD = 64
NH = 16
GROUP = 8
NE = 32
TOPK = 4
CAP = 64
EPS = 1e-5
LIMIT = 7.0
ALPHA = 1.702
SCALE = HD ** -0.5
SLOPES = [2.0 ** (-8.0 * (h + 1) / NH) for h in range(NH)]
NEG = -1e30

EXTRA = T * TOPK // CAP - 1
PASSES = T // CAP
NBLK = NE + EXTRA

SLOTS = 12
PIECE = 2048
COLS = PIECE // C
KPP = PIECE // D
N_GLU, N_Q, N_KV = 2 * D, D, 2 * 2 * HD

GLU_COLS = [off + COLS * i for i in range(D // COLS) for off in (0, D)]
IN_COLS = GLU_COLS + [N_GLU + COLS * i for i in range((N_Q + N_KV + 2 * D) // COLS)]
NZ = len(IN_COLS)
N_GLUP = len(GLU_COLS)
N_QP = N_Q // COLS
KV_PIECE = N_GLUP + N_QP
GATE0 = KV_PIECE + 1
NO = D // COLS
NW = D // (P * KPP)
CONV0 = NZ
ATTN0 = NZ + NO
WOUT0 = NZ + 2 * NO
FRONT = WOUT0 + NW
MPE = 3 * NW

VEC = {}
_row = 0
for _name, _n in (("g_mix", D), ("b_in", N_GLU + N_Q + N_KV + 2 * D), ("conv_b", D), ("conv_ln_g", D),
                  ("conv_ln_b", D), ("b_conv_out", D), ("b_attn_out", D), ("g_ffn", D)):
    VEC[_name] = (_row, _n // P)
    _row += _n // P
VROWS = _row


def build(nc, t_in, out):
    f32, bf16, i32 = mybir.dt.float32, mybir.dt.bfloat16, mybir.dt.int32
    ALU = mybir.AluOpType
    ACT = mybir.ActivationFunctionType
    X = mybir.AxisListType.X

    ctx = ExitStack()
    with ctx:
        def sb(name, shape, dt=f32):
            return ctx.enter_context(nc.sbuf_tensor(name, shape, dt))

        def sem(name):
            return ctx.enter_context(nc.semaphore(name))

        ring = sb("ring", [P, SLOTS, PIECE])
        x = sb("x_tok", [P, TT, D])
        xh = sb("x_normed", [P, TT, D])
        hT = sb("hT", [P, C, T])
        u = sb("u_padded", [P, C, KTAPS - 1 + T])
        cv = sb("conv_out", [P, C, T])
        gates = sb("gates", [P, 2 * C, T])
        qT = sb("qT", [P, C, T])
        kdup = sb("kT_both_halves", [P, 2, T])
        vT = sb("vT", [P, T])
        v = sb("v_tok", [P, TT, P])
        sc = sb("scores", [P, 2, 4, 3 * P])
        pt = sb("probsT", [P, 3, 4 * P])
        sigb = sb("glu_sigmoid", [P, 2, 2, T])
        vrows = sb("vector_rows", [VROWS, P])
        vecs = sb("vectors", [P, VROWS])
        cwrows = sb("conv_w_rows", [KTAPS, D])
        cw = sb("conv_wT", [P, C, KTAPS])
        ident = sb("ident", [P, P])
        ones = sb("ones", [P, P])
        ones_h = sb("ones_bf16", [P, P], bf16)
        before = sb("strictly_before", [P, P], bf16)
        ndist = sb("minus_distance", [P, 2 * P])
        iota = sb("slot_iota", [P, 2, CAP])
        sinks = sb("sinks", [P, NH])
        brt = sb("b_router", [P, NE])
        wrt = sb("w_router", [P, C, NE])
        eps = sb("eps", [P, 1])
        ss = sb("sums_of_squares", [P, 2, TT])
        std = sb("stds", [P, 2, TT])
        rstd = sb("rstds", [P, 2, TT])
        smax = sb("softmax_max", [P, 2, 4])
        sneg = sb("softmax_minus_max", [P, 2, 2, 4])
        ssum = sb("softmax_sum", [P, 2, 2, 4])
        ssnk = sb("softmax_sink", [P, 2, 2, 4])
        sinks8 = sb("sinks_over_scale", [P, NH])
        logits = sb("logits", [P, TT, NE])
        rt = sb("router_work", [P, 6, TT, NE])
        m8 = sb("top8", [P, TT, 8])
        quota = sb("router_small", [P, 4, TT])
        member_h = sb("member_bf16", [P, TT, NE], bf16)
        member = sb("member", [P, TT, NE])
        wts = sb("weights", [P, TT, NBLK + 1])
        rank = sb("ranks", [P, TT, NBLK + 1])
        ehot = sb("expert_onehot", [NE, NBLK + 1])
        epart = sb("expert_of_partition", [NE, 1])
        cnt = sb("expert_counts", [P, NE])
        flag = sb("further_blocks", [P, PASSES - 1, NE])
        nblk_f = sb("n_blocks_f", [P, 2])
        nblk_i = sb("n_blocks", [P, 1], i32)
        eid_i = sb("expert_ids", [P, EXTRA], i32)
        wT = sb("weightsT", [NE, T])

        def over(t, off, *dims):
            flat = t[:].rearrange("p a b -> p (a b)")
            n = 1
            for d in dims:
                n *= d
            ap = flat[:, off:off + n]
            if len(dims) == 2:
                ap = ap.rearrange("p (a b) -> p a b", a=dims[0])
            if len(dims) == 3:
                ap = ap.rearrange("p (a b c) -> p a b c", a=dims[0], b=dims[1])
            return ap

        cen = cv
        sq = over(u, 0, C, T)
        flat = sigb[:].rearrange("p a b c -> p (a b c)")
        ln_means, ln_stds, ln_rstds = (flat[:, k * T:(k + 1) * T] for k in range(3))
        oT = qT
        hfT = hT
        gmin = over(gates, 0, 512)
        sig = over(gates, 512, 512)
        uclip = over(gates, 1024, 512)
        hidden = over(gates, 1536, 512)
        actT = over(gates, 2048, 4, 2, CAP)
        xg = over(gates, 2560, 512)
        xT = over(gates, 3072, 4, 2, CAP)
        yb = over(cv, 0, 512)
        sel = over(cv, 512, TT, CAP)
        selw = over(cv, 640, TT, 2 * CAP)
        swT = over(cv, 896, TT, P)
        bsel = over(cv, 1152, CAP)
        bgu = u
        bgate = over(u, 0, D)
        bup = over(u, D, D)
        bdown = over(qT, 0, D)
        gfin = over(qT, D, D)
        ysum = xh
        tab = over(hT, 0, EXTRA, (PASSES - 1) * NE)
        tab2 = sc[:].rearrange("p a b c -> p (a b c)")[:, 0:EXTRA * (PASSES - 1) * NE].rearrange(
            "p (a b) -> p a b", a=EXTRA)
        rel = pt[:].rearrange("p a b -> p (a b)")[:, 0:(PASSES - 1) * NE].rearrange(
            "p (a b) -> p a b", a=PASSES - 1)
        pos = pt[:].rearrange("p a b -> p (a b)")[:, 96:192]
        blockno = pt[:].rearrange("p a b -> p (a b)")[:, 192:192 + EXTRA]
        eids = pt[:].rearrange("p a b -> p (a b)")[:, 256:256 + EXTRA]
        zero96 = pt[:].rearrange("p a b -> p (a b)")[:, 288:384]
        enum = pt[:].rearrange("p a b -> p (a b)")[:, 384:416]

        bank = [ctx.enter_context(nc.psum_tensor(f"bank{i}", [P, 512], f32)) for i in range(8)]
        Y = [[bank[2 * t + h] for h in range(2)] for t in range(TT)]
        A, B, G, DN = bank[4], bank[5], bank[6], bank[7]

        x_loaded, vecs_loaded, small_loaded, k_swapped = sem("x_loaded"), sem("vecs_loaded"), sem("small_loaded"), sem("k_swapped")
        moe_loaded, out_stored = sem("moe_loaded"), sem("out_stored")
        slot_full = [sem(f"slot_full{i}") for i in range(SLOTS)]
        piece_done = sem("piece_done")
        consts = sem("consts")
        u_zero, u_ready = sem("u_zero"), sem("u_ready")
        squares, stds = sem("squares"), sem("stds")
        z_out, gates_on = sem("z_out"), sem("gates_on")
        ln_sq, ln_std, ln_sig = sem("ln_sq"), sem("ln_std"), sem("ln_sig")
        exps, pt_out, ot_out = sem("exps"), sem("pt_out"), sem("ot_out")
        vecsT, cwT, xTp = sem("vecsT"), sem("cwT"), sem("xTp")
        vtr, s_done, pt_done, pv_done, ln_mean, ln_var = (sem("vtr"), sem("s_done"), sem("pt_done"), sem("pv_done"),
                                                          sem("ln_mean"), sem("ln_var"))
        hfT_done, logit_done, rank_done = sem("hfT_done"), sem("logit_done"), sem("rank_done")
        dve = sem("dve_step")
        vecs_out, cw_out, xh_ready, hT_ready, v_out = sem("vecs_out"), sem("cw_out"), sem("xh_ready"), sem("hT_ready"), sem("v_out")
        taps = sem("taps")
        s_masked, p_ready = sem("s_masked"), sem("p_ready")
        ln_cen, ln_z, silu_ready = sem("ln_cen"), sem("ln_z"), sem("silu_ready")
        y_out, mixed_ready, xnew_ready = sem("y_out"), sem("mixed_ready"), sem("xnew_ready")
        hfT_ready, le_ready, member_ready, rtr_ready, wT_out = (sem("hfT_ready"), sem("le_ready"), sem("member_ready"),
                                                                sem("rtr_ready"), sem("wT_out"))
        le_exp = sem("le_exp")
        n_ready, ov_ready, ov_step = sem("n_ready"), sem("ov_ready"), sem("ov_step")
        sel_ready, gathered, xg_out, xT_done, xT_ready = sem("sel_ready"), sem("gathered"), sem("xg_out"), sem("xT_done"), sem("xT_ready")
        selw_ready, swT_done, swT_out = sem("selw_ready"), sem("swT_done"), sem("swT_out")
        gmin_ready, sig_ready, act_steps, act_ready = sem("gmin_ready"), sem("sig_ready"), sem("act_steps"), sem("act_ready")
        actT_done, actT_out, yb_out = sem("actT_done"), sem("actT_out"), sem("yb_out")
        y_done, ysum_ready = sem("y_done"), sem("ysum_ready")

        def vec(name, c, rows=slice(0, P)):
            return vecs[rows, VEC[name][0] + c:VEC[name][0] + c + 1]

        def by_cols(n):
            return ring[:, n % SLOTS, :].rearrange("p (c n) -> p c n", c=C)

        def by_rows(n):
            return ring[:, n % SLOTS, :].rearrange("p (k n) -> p k n", k=KPP)

        def arrived(eng, n, later=0):
            eng.wait_ge(slot_full[n % SLOTS], 16 * (n // SLOTS + 1) + 16 * later)

        block = ctx.enter_context(nc.Block())

        @block.sync
        def _(sp):
            sp.dma_start(x[:], t_in["x"].rearrange("a (t p) d -> p (a t) d", p=P)).then_inc(x_loaded, 16)

            def fetch(n, dst, src):
                if n >= SLOTS:
                    sp.wait_ge(piece_done, n - SLOTS + 1)
                sp.dma_start(dst, src).then_inc(slot_full[n % SLOTS], 16)

            w_in = t_in["w_in"].rearrange("(c p) n -> p c n", p=P)
            for n, col in enumerate(IN_COLS):
                fetch(n, by_cols(n), w_in[:, :, col:col + COLS])
            for first, name in ((CONV0, "w_conv_out"), (ATTN0, "w_attn_out")):
                w = t_in[name].rearrange("(c p) n -> p c n", p=P)
                for i in range(NO):
                    fetch(first + i, by_cols(first + i), w[:, :, COLS * i:COLS * (i + 1)])
            w = t_in["w_out"].rearrange("(i k p) n -> i p k n", p=P, k=KPP)
            for i in range(NW):
                fetch(WOUT0 + i, by_rows(WOUT0 + i), w[i])

            def expert_pieces(b, e):
                for j in range(MPE):
                    w = t_in[("w_gate", "w_up", "w_down")[j // NW]].rearrange("e (i k p) n -> e i p k n", p=P, k=KPP)
                    sp.wait_ge(piece_done, b * MPE + FRONT + j - SLOTS + 1)
                    sp.dma_start(by_rows(FRONT + j), w[bass.ds(e, 1), j % NW].rearrange("a p k n -> p (a k) n")).then_inc(
                        slot_full[(FRONT + j) % SLOTS], 16)

            with sp.Fori(0, NE) as b:
                expert_pieces(b, b)
            sp.wait_ge(n_ready, 1)
            n_blocks = sp.value_load(nblk_i[0:1, 0:1], min_val=NE, max_val=NBLK)
            with sp.Fori(NE, NBLK) as b:
                with sp.If(b < n_blocks):
                    sp.wait_ge(ov_ready, 1)
                    e = sp.value_load(eid_i[0:1, bass.ds(b - NE, 1)], min_val=0, max_val=NE - 1)
                    expert_pieces(b, e)
            for t in range(TT):
                sp.wait_ge(ysum_ready, t + 1)
                sp.dma_start(out[0, t * P:(t + 1) * P, :], ysum[:, t, :]).then_inc(out_stored, 16)
            sp.wait_ge(out_stored, 16 * TT)

        @block.gpsimd
        def _(pool):
            own = [0]

            def step(ins):
                own[0] += 1
                ins.then_inc(consts, 1)
                pool.wait_ge(consts, own[0])

            step(pool.memset(ident[:], 0.0))
            step(pool.affine_select(out=ident[:], in_=ident[:], compare_op=ALU.not_equal, fill=1.0, base=0,
                                    pattern=[[-1, P]], channel_multiplier=1))
            step(pool.memset(eps[:], EPS))
            assert own[0] == 3
            pool.memset(u[:, :, 0:KTAPS - 1], 0.0).then_inc(u_zero, 1)
            step(pool.memset(ones[:], 1.0))
            step(pool.memset(ones_h[:], 1.0))
            step(pool.memset(before[:], 1.0))
            step(pool.affine_select(out=before[:], in_=before[:], compare_op=ALU.is_gt, fill=0.0, base=0,
                                    pattern=[[1, P]], channel_multiplier=-1))
            step(pool.iota(ndist[:], pattern=[[1, 2 * P]], base=-P, channel_multiplier=-1,
                           allow_small_or_imprecise_dtypes=True))
            step(pool.affine_select(out=ndist[:], in_=ndist[:], compare_op=ALU.is_ge, fill=NEG, base=P,
                                    pattern=[[-1, 2 * P]], channel_multiplier=1))
            step(pool.affine_select(out=ndist[:], in_=ndist[:], compare_op=ALU.is_ge, fill=NEG, base=-1,
                                    pattern=[[1, 2 * P]], channel_multiplier=-1))
            step(pool.iota(iota[:], pattern=[[0, 2], [1, CAP]], base=0, channel_multiplier=0,
                           allow_small_or_imprecise_dtypes=True))
            step(pool.iota(epart[:], pattern=[[0, 1]], base=0, channel_multiplier=1,
                           allow_small_or_imprecise_dtypes=True))
            step(pool.memset(rank[:], -1.0))
            step(pool.memset(wts[:], 0.0))
            step(pool.memset(ehot[:], 0.0))
            step(pool.affine_select(out=ehot[:, 0:NE], in_=ehot[:, 0:NE], compare_op=ALU.not_equal, fill=1.0, base=0,
                                    pattern=[[-1, NE]], channel_multiplier=1))
            pool.wait_ge(u_zero, 1)
            for i in range(N_GLUP // 2):
                pool.wait_ge(z_out, 2 * i + 2)
                pool.tensor_tensor(u[:, 2 * i:2 * i + 2, KTAPS - 1:], u[:, 2 * i:2 * i + 2, KTAPS - 1:],
                                   sigb[:, i % 2], ALU.mult).then_inc(u_ready, 1)
            pool.wait_ge(piece_done, CONV0 + NO)
            pool.memset(yb, 0.0).then_inc(yb_out, 1)
            pool.memset(swT, 0.0).then_inc(swT_out, 1)

        @block.scalar
        def _(act):
            for name, (row, n) in VEC.items():
                act.dma_start(vrows[row:row + n, :], t_in[name].rearrange("(c p) -> c p", p=P)).then_inc(vecs_loaded, 16)
            act.dma_start(cwrows[:], t_in["conv_w"]).then_inc(vecs_loaded, 16)
            act.dma_start(sinks[:], t_in["attn_sinks"].partition_broadcast(P)).then_inc(small_loaded, 16)
            act.dma_start(brt[:], t_in["b_router"].partition_broadcast(P)).then_inc(small_loaded, 16)
            act.dma_start(wrt[:], t_in["w_router"].rearrange("(c p) e -> p c e", p=P)).then_inc(small_loaded, 16)

            def token_stds(k, junk, data, ready, count):
                for t in range(TT):
                    act.wait_ge(ready, count(t))
                    act.activation(junk[:, t, :], data[:, t, :], ACT.Square, accum_out=ss[:, k, t:t + 1]).then_inc(squares, 1)
                act.wait_ge(squares, (k + 1) * TT)
                act.activation(std[:, k, :], ss[:, k, :], ACT.Sqrt, scale=1.0 / D, bias=eps[:, 0:1]).then_inc(stds, 1)

            act.wait_ge(consts, 3)
            token_stds(0, xh, x, x_loaded, lambda t: 16)

            act.wait_ge(vecs_out, 1)

            def evacuate(n, dst, func=ACT.Identity):
                act.wait_ge(piece_done, n + 1)
                for j in range(2):
                    last = act.activation(dst[j], bank[n % 3][:, j * T:(j + 1) * T], func,
                                          bias=vec("b_in", IN_COLS[n] // P + j))
                return last.then_inc(z_out, 1)

            for i in range(N_GLUP // 2):
                evacuate(2 * i, [u[:, 2 * i + j, KTAPS - 1:] for j in range(2)])
                if i >= 2:
                    act.wait_ge(u_ready, i - 1)
                act.wait_ge(piece_done, 2 * i + 2)
                for j in range(2):
                    last = act.activation(sigb[:, i % 2, j, :], bank[(2 * i + 1) % 3][:, j * T:(j + 1) * T], ACT.Sigmoid,
                                          bias=vec("b_in", IN_COLS[2 * i + 1] // P + j))
                last.then_inc(z_out, 1)
            for i in range(N_QP):
                evacuate(N_GLUP + i, [qT[:, 2 * i + j, :] for j in range(2)])
            act.wait_ge(piece_done, KV_PIECE + 1)
            for g in range(2):
                rows = slice(g * HD, (g + 1) * HD)
                act.activation(kdup[rows, g, :], bank[KV_PIECE % 3][rows, 0:T], ACT.Identity,
                               bias=vec("b_in", IN_COLS[KV_PIECE] // P, rows))
            act.activation(vT[:], bank[KV_PIECE % 3][:, T:2 * T], ACT.Identity,
                           bias=vec("b_in", IN_COLS[KV_PIECE] // P + 1)).then_inc(z_out, 1)
            act.wait_ge(z_out, KV_PIECE + 1)
            for g in range(2):
                act.dma_start(kdup[(1 - g) * HD:(2 - g) * HD, g, :], kdup[g * HD:(g + 1) * HD, g, :]).then_inc(k_swapped, 16)

            def gate_piece(i):
                evacuate(GATE0 + i, [gates[:, 2 * i + j, :] for j in range(2)])

            for i in range(6):
                gate_piece(i)
            act.wait_ge(ln_cen, 1)
            act.wait_ge(u_ready, N_GLUP // 2)
            act.activation(sq, cen[:], ACT.Square).then_inc(ln_sq, 1)
            for i in range(6, NZ - GATE0):
                gate_piece(i)
            act.wait_ge(ln_var, 1)
            act.activation(ln_stds, bank[7][:, 0:T], ACT.Sqrt, scale=1.0 / D, bias=eps[:, 0:1]).then_inc(ln_std, 1)
            act.wait_ge(ln_z, 1)
            act.activation(sq, cen[:], ACT.Sigmoid).then_inc(ln_sig, 1)
            act.wait_ge(z_out, NZ)
            act.activation(gates[:], gates[:], ACT.Sigmoid).then_inc(gates_on, 1)

            def transposed_probs(q):
                if q >= 1:
                    act.wait_ge(pv_done, q)
                for k in range(3):
                    act.wait_ge(pt_done, 3 * q + k + 1)
                    act.activation(pt[:, k, :], bank[6 + (3 * q + k) % 2][:], ACT.Copy).then_inc(pt_out, 1)
                act.wait_ge(pv_done, q + 1)
                g, par = q // 2, q % 2
                rows = slice(par * HD, (par + 1) * HD)
                for n in range(TT):
                    last = act.activation(oT[rows, 4 * g:4 * g + 4, n * P:(n + 1) * P],
                                          bank[3 + n][rows, :].rearrange("p (j q) -> p j q", j=4), ACT.Copy)
                last.then_inc(ot_out, 1)

            for q in range(4):
                act.wait_ge(s_masked, q + 1)
                g, par = q // 2, q % 2
                for j in range(4):
                    for n, (lo, hi) in enumerate(((0, P), (P, 3 * P))):
                        act.activation(sc[:, q % 2, j, lo:hi], sc[:, q % 2, j, lo:hi], ACT.Exp, scale=SCALE,
                                       bias=sneg[:, q % 2, n, j:j + 1], accum_out=ssum[:, q % 2, n, j:j + 1])
                act.activation(ssnk[:, q % 2], ssnk[:, q % 2], ACT.Exp).then_inc(exps, 1)
                if q >= 1:
                    transposed_probs(q - 1)
            transposed_probs(3)

            token_stds(1, xh, x, xnew_ready, lambda t: t + 1)
            act.wait_ge(le_ready, 1)
            act.activation(rt[:, 4], rt[:, 4], ACT.Exp).then_inc(le_exp, 1)
            act.dma_start(bgate[0:NE, :], t_in["b_gate"]).then_inc(moe_loaded, 16)
            act.dma_start(bup[0:NE, :], t_in["b_up"]).then_inc(moe_loaded, 16)
            act.dma_start(bdown[0:NE, :], t_in["b_down"]).then_inc(moe_loaded, 16)
            act.dma_start(gfin, t_in["g_final"].partition_broadcast(P)).then_inc(moe_loaded, 16)

            def copy_xg(k):
                act.wait_ge(gathered, k + 1)
                act.activation(xg, G[:], ACT.Copy).then_inc(xg_out, 1)

            def moe_block(b, off):
                act.wait_ge(gmin_ready, b + 1)
                act.activation(sig, gmin, ACT.Sigmoid, scale=ALPHA).then_inc(sig_ready, 1)
                copy_xg(b + (off + 1))
                act.wait_ge(actT_done, b + 1)
                act.activation(actT, A[:].rearrange("p (k h s) -> p k h s", k=4, h=2), ACT.Copy).then_inc(actT_out, 1)
                act.wait_ge(swT_done, b + 2)
                act.activation(swT, B[:, 0:T].rearrange("p (t s) -> p t s", t=TT), ACT.Copy).then_inc(swT_out, 1)
                act.wait_ge(piece_done, b * MPE + (FRONT + 3 * NW))
                act.activation(yb, DN[:], ACT.Copy).then_inc(yb_out, 1)

            copy_xg(0)
            with act.Fori(0, NE) as b:
                moe_block(b, 0)
            act.wait_ge(n_ready, 1)
            n_blocks = act.value_load(nblk_i[0:1, 0:1], min_val=NE, max_val=NBLK)
            with act.If(NE < n_blocks):
                copy_xg(NE + 1)
            with act.Fori(NE, NBLK) as b:
                with act.If(b < n_blocks):
                    moe_block(b, 1)
            for t in range(TT):
                act.wait_ge(xnew_ready, TT + t + 1)
                act.activation(xh[:, t, :], x[:, t, :], ACT.Square, accum_out=ss[:, 0, t:t + 1]).then_inc(squares, 1)
            act.wait_ge(squares, 3 * TT)
            act.activation(std[:, 0, :], ss[:, 0, :], ACT.Sqrt, scale=1.0 / D, bias=eps[:, 0:1]).then_inc(stds, 1)

        @block.vector
        def _(dv):
            own = [0]

            def step(ins):
                own[0] += 1
                ins.then_inc(dve, 1)
                dv.wait_ge(dve, own[0])

            dv.wait_ge(vecsT, 1)
            dv.tensor_copy(vecs[:], bank[6][:, 0:VROWS]).then_inc(vecs_out, 1)
            dv.wait_ge(vecs_out, 1)
            dv.wait_ge(cwT, 1)
            dv.tensor_copy(cw[:], bank[7][:, 0:C * KTAPS].rearrange("p (c k) -> p c k", c=C)).then_inc(cw_out, 1)
            dv.wait_ge(small_loaded, 48)
            step(dv.tensor_scalar(sinks8[:], sinks[:], 1.0 / SCALE, None, ALU.mult))
            dv.wait_ge(stds, 1)
            step(dv.reciprocal(rstd[:, 0, :], std[:, 0, :]))
            for t in range(TT):
                dv.tensor_scalar(xh[:, t, :], x[:, t, :], rstd[:, 0, t:t + 1], None, ALU.mult).then_inc(xh_ready, 1)
            g0 = VEC["g_mix"][0]
            for i in range(4):
                dv.wait_ge(xTp, i + 1)
                dv.tensor_tensor(hT[:, 2 * i:2 * i + 2, :], bank[i][:].rearrange("p (c t) -> p c t", c=2),
                                 vecs[:, g0 + 2 * i:g0 + 2 * i + 2].unsqueeze(2).to_broadcast([P, 2, T]),
                                 ALU.mult).then_inc(hT_ready, 1)

            cb = VEC["conv_b"][0]
            dv.wait_ge(cw_out, 1)
            with dv.Fori(0, C // 2) as i:
                dv.wait_ge(u_ready, i + 1)
                for k in range(KTAPS):
                    for j in range(2):
                        src = u[:, bass.ds(2 * i + j, 1), k:k + T].rearrange("p a t -> p (a t)")
                        dst = cv[:, bass.ds(2 * i + j, 1), :].rearrange("p a t -> p (a t)")
                        w = cw[:, bass.ds(2 * i + j, 1), k:k + 1].rearrange("p a t -> p (a t)")
                        if k == 0:
                            ins = dv.tensor_scalar(dst, src, w, vecs[:, bass.ds(cb + 2 * i + j, 1)], ALU.mult, ALU.add)
                        else:
                            dv.wait_ge(taps, 2 * KTAPS * i + 2 * k + j - 1)
                            ins = dv.scalar_tensor_tensor(dst, src, w, dst, ALU.mult, ALU.add)
                        ins.then_inc(taps, 1)
            dv.wait_ge(taps, C * KTAPS)

            def mask_and_max(q):
                g, par = q // 2, q % 2
                h0 = g * GROUP + par
                dv.wait_ge(s_done, q + 1)
                if q == 0:
                    dv.wait_ge(consts, 10)
                if q >= 2:
                    dv.wait_ge(pt_done, 3 * (q - 1))
                for j in range(4):
                    slope = SLOPES[h0 + 2 * j] / SCALE
                    dv.scalar_tensor_tensor(sc[:, q % 2, j, 0:P], ndist[:, P:2 * P], slope,
                                            bank[3][:, j * P:(j + 1) * P], ALU.mult, ALU.add)
                    last = dv.scalar_tensor_tensor(sc[:, q % 2, j, P:3 * P], ndist[:], slope,
                                                   bank[4 + j // 2][:, (j % 2) * T:(j % 2 + 1) * T], ALU.mult, ALU.add)
                step(last)
                dv.reduce_max(smax[:, 0, :], sc[:, q % 2, :, 0:P], axis=X)
                step(dv.reduce_max(smax[:, 1, :], sc[:, q % 2, :, P:3 * P], axis=X))
                snk = sinks8[:, h0:h0 + 7:2].unsqueeze(1).to_broadcast([P, 2, 4])
                step(dv.tensor_tensor(smax[:], smax[:], snk, ALU.max))
                step(dv.tensor_scalar(sneg[:, q % 2], smax[:], -SCALE, None, ALU.mult))
                snk = sinks[:, h0:h0 + 7:2].unsqueeze(1).to_broadcast([P, 2, 4])
                dv.tensor_tensor(ssnk[:, q % 2], sneg[:, q % 2], snk, ALU.add).then_inc(s_masked, 1)

            def divide(q):
                dv.wait_ge(exps, q + 1)
                step(dv.tensor_tensor(ssum[:, q % 2], ssum[:, q % 2], ssnk[:, q % 2], ALU.add))
                step(dv.reciprocal(ssum[:, q % 2], ssum[:, q % 2]))
                for n, (lo, hi) in enumerate(((0, P), (P, 3 * P))):
                    last = dv.tensor_tensor(sc[:, q % 2, :, lo:hi], sc[:, q % 2, :, lo:hi],
                                            ssum[:, q % 2, n, :].unsqueeze(2).to_broadcast([P, 4, hi - lo]), ALU.mult)
                last.then_inc(p_ready, 1)

            def out_piece(k, i):
                n = (CONV0, ATTN0)[k] + i
                dv.wait_ge(piece_done, n + 1)
                dv.wait_ge(gates_on, 1)
                for j in range(2):
                    c = 2 * i + j
                    last = dv.scalar_tensor_tensor(gates[:, k * C + c, :], bank[n % 3][:, j * T:(j + 1) * T],
                                                   vec(("b_conv_out", "b_attn_out")[k], c), gates[:, k * C + c, :],
                                                   ALU.add, ALU.mult)
                last.then_inc(y_out, 1)

            def further_blocks():
                NP = PASSES - 1
                own = [0]

                def step(ins):
                    own[0] += 1
                    ins.then_inc(ov_step, 1)
                    dv.wait_ge(ov_step, own[0])

                dv.memset(zero96, 0.0)
                for i in range(EXTRA):
                    dv.memset(blockno[:, i:i + 1], float(i + 1))
                for e in range(NE):
                    last = dv.memset(enum[:, e:e + 1], float(e))
                step(last)
                ff = flag[:].rearrange("p a b -> p (a b)")
                step(dv.tensor_tensor_scan(pos, ff, zero96, 0.0, ALU.add, ALU.add))
                step(dv.tensor_tensor(tab, pos.unsqueeze(1).to_broadcast([P, EXTRA, NP * NE]),
                                      blockno.unsqueeze(2).to_broadcast([P, EXTRA, NP * NE]), ALU.is_equal))
                step(dv.tensor_tensor(tab, tab, ff.unsqueeze(1).to_broadcast([P, EXTRA, NP * NE]), ALU.mult))

                def picked(dst, values):
                    step(dv.tensor_tensor(tab2, tab, values.unsqueeze(1).to_broadcast([P, EXTRA, NP * NE]), ALU.mult))
                    step(dv.reduce_sum(dst, tab2, axis=X))

                relf = rel.rearrange("p a b -> p (a b)")
                for t in range(TT):
                    for k in range(NP):
                        last = dv.tensor_scalar(rel[:, k, :], rank[:, t, 0:NE], -float(CAP * (k + 1)), None, ALU.add)
                    step(last)
                    picked(rank[:, t, NE:NBLK], relf)
                    for k in range(NP):
                        last = dv.tensor_copy(rel[:, k, :], wts[:, t, 0:NE])
                    step(last)
                    picked(wts[:, t, NE:NBLK], relf)
                for k in range(NP):
                    last = dv.tensor_copy(rel[:, k, :], enum)
                step(last)
                picked(eids, relf)
                step(dv.tensor_scalar(ehot[:, NE:NBLK], eids[0:NE, :], epart[:, 0:1], None, ALU.is_equal))
                dv.tensor_copy(eid_i[:], eids).then_inc(ov_ready, 1)

            dv.wait_ge(vtr, 1)
            dv.tensor_copy(v[:], bank[6][:, 0:T].rearrange("p (t c) -> p t c", t=TT)).then_inc(v_out, 1)
            mask_and_max(0)
            dv.wait_ge(ln_mean, 1)
            step(dv.tensor_scalar(ln_means, bank[6][:, 0:T], 1.0 / D, None, ALU.mult))
            dv.tensor_tensor(cen[:], cv[:], ln_means.unsqueeze(1).to_broadcast([P, C, T]), ALU.subtract).then_inc(ln_cen, 1)
            dv.wait_ge(ln_std, 1)
            step(dv.reciprocal(ln_rstds, ln_stds))
            step(dv.tensor_tensor(cen[:], cen[:], ln_rstds.unsqueeze(1).to_broadcast([P, C, T]), ALU.mult))
            for c in range(C):
                last = dv.tensor_scalar(cen[:, c, :], cen[:, c, :], vec("conv_ln_g", c), vec("conv_ln_b", c), ALU.mult, ALU.add)
            last.then_inc(ln_z, 1)
            dv.wait_ge(ln_sig, 1)
            dv.tensor_tensor(cen[:], cen[:], sq, ALU.mult).then_inc(silu_ready, 1)

            for q in range(4):
                divide(q)
                if q < 3:
                    mask_and_max(q + 1)
                out_piece(0, q)
            for i in range(NO):
                out_piece(1, i)
                dv.wait_ge(y_out, NO + i + 1)
                dv.tensor_tensor(gates[:, 2 * i:2 * i + 2, :], gates[:, 2 * i:2 * i + 2, :],
                                 gates[:, C + 2 * i:C + 2 * i + 2, :], ALU.add).then_inc(mixed_ready, 1)

            dv.wait_ge(piece_done, FRONT)
            for t in range(TT):
                for h in range(2):
                    last = dv.tensor_tensor(x[:, t, h * 512:(h + 1) * 512], x[:, t, h * 512:(h + 1) * 512],
                                            bank[3 + 2 * t + h][:], ALU.add)
                last.then_inc(xnew_ready, 1)
            dv.wait_ge(stds, 2)
            step(dv.reciprocal(rstd[:, 1, :], std[:, 1, :]))
            for t in range(TT):
                dv.tensor_scalar(xh[:, t, :], x[:, t, :], rstd[:, 1, t:t + 1], None, ALU.mult).then_inc(xh_ready, 1)
            g1 = VEC["g_ffn"][0]
            for i in range(4):
                dv.wait_ge(hfT_done, i + 1)
                dv.tensor_tensor(hfT[:, 2 * i:2 * i + 2, :], bank[(0, 1, 2, 7)[i]][:].rearrange("p (c t) -> p c t", c=2),
                                 vecs[:, g1 + 2 * i:g1 + 2 * i + 2].unsqueeze(2).to_broadcast([P, 2, T]),
                                 ALU.mult).then_inc(hfT_ready, 1)

            L, gt, eq, cum, le, tmp = logits[:], rt[:, 0], rt[:, 1], rt[:, 2], rt[:, 4], rt[:, 5]
            dv.wait_ge(logit_done, 1)
            step(dv.tensor_tensor(L, bank[3][:, 0:TT * NE].rearrange("p (t e) -> p t e", t=TT),
                                  brt[:].unsqueeze(1).to_broadcast([P, TT, NE]), ALU.add))
            dv.max(m8[:, 0, :], L[:, 0, :])
            step(dv.max(m8[:, 1, :], L[:, 1, :]))
            dv.tensor_tensor(le, L, m8[:, :, 0:1].to_broadcast([P, TT, NE]), ALU.subtract).then_inc(le_ready, 1)
            fourth = m8[:, :, TOPK - 1:TOPK].to_broadcast([P, TT, NE])
            dv.tensor_tensor(eq, L, fourth, ALU.is_equal)
            step(dv.tensor_tensor(gt, L, fourth, ALU.is_gt))
            for t in range(TT):
                step(dv.tensor_tensor_scan(cum[:, t, :], eq[:, t, :], eq[:, t, :], 0.0, ALU.add, ALU.max))
            step(dv.reduce_sum(quota[:, 0, :], gt, axis=X))
            step(dv.tensor_tensor(cum, cum, quota[:, 0, :].unsqueeze(2).to_broadcast([P, TT, NE]), ALU.add))
            step(dv.scalar_tensor_tensor(tmp, cum, float(TOPK), eq, ALU.is_le, ALU.mult))
            step(dv.tensor_tensor(member[:], gt, tmp, ALU.add))
            dv.tensor_copy(member_h[:], member[:]).then_inc(member_ready, 1)
            dv.wait_ge(le_exp, 1)
            step(dv.tensor_tensor(le, le, member[:], ALU.mult))
            step(dv.reduce_sum(quota[:, 1, :], le, axis=X))
            step(dv.reciprocal(quota[:, 2, :], quota[:, 1, :]))
            dv.wait_ge(consts, 16)
            step(dv.tensor_tensor(wts[:, :, 0:NE], le, quota[:, 2, :].unsqueeze(2).to_broadcast([P, TT, NE]), ALU.mult))
            dv.wait_ge(rank_done, 1)
            step(dv.scalar_tensor_tensor(tmp, bank[4][:, 0:TT * NE].rearrange("p (t e) -> p t e", t=TT), 1.0, member[:],
                                         ALU.add, ALU.mult))
            step(dv.tensor_scalar(rank[:, :, 0:NE], tmp, -1.0, None, ALU.add))
            dv.tensor_copy(cnt[:], bank[4][:, TT * NE:(TT + 1) * NE]).then_inc(rtr_ready, 1)

            def select(b, k):
                if not isinstance(k, int) or k > 0:
                    dv.wait_ge(gathered, k)
                for t in range(TT):
                    last = dv.tensor_scalar(sel[:, t, :], iota[:, 0, :], rank[:, t, bass.ds(b, 1)], None, ALU.is_equal)
                last.then_inc(sel_ready, 1)

            def tokensT(b, k):
                dv.wait_ge(xT_done, k + 1)
                dv.tensor_scalar(bsel[0:NE, :], ones[0:NE, 0:CAP], ehot[:, bass.ds(b, 1)], None, ALU.mult)
                ge = vecs[:, g1:g1 + C].rearrange("p (h k) -> p k h", h=2).unsqueeze(3).to_broadcast([P, 4, 2, CAP])
                dv.tensor_tensor(xT, G[:].rearrange("p (k h s) -> p k h s", k=4, h=2), ge, ALU.mult).then_inc(xT_ready, 1)

            def moe_block(b, off):
                select(b + 1, b + (off + 1))
                dv.wait_ge(swT_done, b + 1)
                for t in range(TT):
                    last = dv.tensor_scalar(selw[:, t, :], iota[:].rearrange("p a s -> p (a s)"), rank[:, t, bass.ds(b, 1)],
                                            wts[:, t, bass.ds(b, 1)], ALU.is_equal, ALU.mult)
                last.then_inc(selw_ready, 1)
                dv.wait_ge(piece_done, b * MPE + (FRONT + NW))
                dv.tensor_scalar(gmin, A[:], LIMIT, None, ALU.min).then_inc(gmin_ready, 1)
                dv.wait_ge(sig_ready, b + 1)
                dv.tensor_tensor(gmin, gmin, sig, ALU.mult).then_inc(act_steps, 1)
                dv.wait_ge(piece_done, b * MPE + (FRONT + 2 * NW))
                dv.tensor_scalar(uclip, B[:], LIMIT, -LIMIT, ALU.min, ALU.max).then_inc(act_steps, 1)
                dv.wait_ge(act_steps, 2 * b + 2)
                dv.scalar_tensor_tensor(hidden, uclip, 1.0, gmin, ALU.add, ALU.mult).then_inc(act_ready, 1)
                tokensT(b + 1, b + (off + 1))

            select(0, 0)
            dv.wait_ge(rtr_ready, 1)
            for k in range(1, PASSES):
                last = dv.tensor_scalar(flag[:, k - 1, :], cnt[:], float(CAP * k), None, ALU.is_gt)
            step(last)
            step(dv.reduce_sum(nblk_f[:, 0:1], flag[:].rearrange("p a b -> p (a b)"), axis=X))
            dv.tensor_scalar(nblk_i[:], nblk_f[:, 0:1], float(NE), None, ALU.add).then_inc(n_ready, 1)
            dv.wait_ge(swT_done, 1)
            dv.tensor_copy(wT[:], bank[5][0:NE, 0:T]).then_inc(wT_out, 1)
            tokensT(0, 0)
            with dv.Fori(0, NE) as b:
                moe_block(b, 0)

            n_blocks = dv.value_load(nblk_i[0:1, 0:1], min_val=NE, max_val=NBLK)
            with dv.If(NE < n_blocks):
                further_blocks()
                select(NE, NE + 1)
                tokensT(NE, NE + 1)
            with dv.Fori(NE, NBLK) as b:
                with dv.If(b < n_blocks):
                    moe_block(b, 1)

            dv.wait_ge(y_done, 1)
            for t in range(TT):
                for h in range(2):
                    last = dv.tensor_tensor(x[:, t, h * 512:(h + 1) * 512], x[:, t, h * 512:(h + 1) * 512], Y[t][h][:], ALU.add)
                last.then_inc(xnew_ready, 1)
            dv.wait_ge(stds, 3)
            dv.reciprocal(rstd[:, 0, :], std[:, 0, :]).then_inc(vecs_out, 1)
            dv.wait_ge(vecs_out, 2)
            for t in range(TT):
                dv.scalar_tensor_tensor(ysum[:, t, :], x[:, t, :], rstd[:, 0, t:t + 1], gfin, ALU.mult, ALU.mult).then_inc(ysum_ready, 1)


        @block.tensor
        def _(pe):
            pe.wait_ge(consts, 2)
            pe.wait_ge(vecs_loaded, 16 * (len(VEC) + 1))
            pe.transpose(bank[6][:, 0:VROWS], vrows[:], ident[0:VROWS, 0:VROWS]).then_inc(vecsT, 1)
            for c in range(C):
                last = pe.transpose(bank[7][:, c * KTAPS:(c + 1) * KTAPS], cwrows[:, c * P:(c + 1) * P],
                                    ident[0:KTAPS, 0:KTAPS])
            last.then_inc(cwT, 1)

            def transpose_x(banks, done):
                for i in range(4):
                    for j in range(2):
                        for t in range(TT):
                            c = 2 * i + j
                            last = pe.transpose(bank[banks[i]][:, j * T + t * P:j * T + (t + 1) * P],
                                                xh[:, t, c * P:(c + 1) * P], ident[:])
                    last.then_inc(done, 1)

            pe.wait_ge(xh_ready, TT)
            transpose_x((0, 1, 2, 3), xTp)
            pe.wait_ge(hT_ready, 4)

            def project(n, src):
                arrived(pe, n)
                if n >= 3:
                    m = n - 3
                    if m < NZ:
                        pe.wait_ge(z_out, m + 1)
                    else:
                        pe.wait_ge(y_out, m - NZ + 1)
                w = by_cols(n)
                for j in range(2):
                    for c in range(C):
                        last = pe.matmul(bank[n % 3][:, j * T:(j + 1) * T], w[:, c, j * P:(j + 1) * P], src[:, c, :],
                                         start=(c == 0), stop=(c == C - 1))
                last.then_inc(piece_done, 1)

            def scores(q):
                g, par = q // 2, q % 2
                rows = slice(par * HD, (par + 1) * HD)
                if q == 0:
                    pe.wait_ge(k_swapped, 32)
                else:
                    pe.wait_ge(s_masked, q)
                if q >= 2:
                    pe.wait_ge(ot_out, q - 1)
                for j in range(4):
                    pe.matmul(bank[3][:, j * P:(j + 1) * P], qT[rows, 4 * g + j, 0:P], kdup[rows, g, 0:P],
                              start=True, stop=True)
                for j in range(4):
                    last = pe.matmul(bank[4 + j // 2][:, (j % 2) * T:(j % 2 + 1) * T], qT[rows, 4 * g + j, P:T],
                                     kdup[rows, g, :], start=True, stop=True)
                last.then_inc(s_done, 1)

            def attend(q):
                g, par = q // 2, q % 2
                rows = slice(par * HD, (par + 1) * HD)
                pe.wait_ge(p_ready, q + 1)
                for k in range(3):
                    if 3 * q + k >= 2:
                        pe.wait_ge(pt_out, 3 * q + k - 1)
                    for j in range(4):
                        last = pe.transpose(bank[6 + (3 * q + k) % 2][:, j * P:(j + 1) * P],
                                            sc[:, q % 2, j, k * P:(k + 1) * P], ident[:])
                    last.then_inc(pt_done, 1)
                if q < 3:
                    pe.wait_ge(s_masked, q + 2)
                pe.wait_ge(pt_out, 3 * q + 3)
                kv = slice(g * HD, (g + 1) * HD)
                pe.matmul(bank[3][rows, :], v[:, 0, kv], pt[:, 0, :], start=True, stop=True)
                pe.matmul(bank[4][rows, :], v[:, 0, kv], pt[:, 1, :], start=True, stop=False)
                pe.matmul(bank[4][rows, :], v[:, 1, kv], pt[:, 2, :], start=False, stop=True).then_inc(pv_done, 1)

            for n in range(GATE0):
                project(n, hT)
            pe.wait_ge(z_out, GATE0)
            pe.wait_ge(cw_out, 1)
            for t in range(TT):
                last = pe.transpose(bank[6][:, t * P:(t + 1) * P], vT[:, t * P:(t + 1) * P], ident[:])
            last.then_inc(vtr, 1)
            scores(0)
            for n in range(GATE0, GATE0 + 6):
                project(n, hT)
            pe.wait_ge(taps, C * KTAPS)
            pe.wait_ge(v_out, 1)
            for c in range(C):
                last = pe.matmul(bank[6][:, 0:T], ones[:], cv[:, c, :], start=(c == 0), stop=(c == C - 1))
            last.then_inc(ln_mean, 1)
            for n in range(GATE0 + 6, NZ):
                project(n, hT)
            pe.wait_ge(ln_sq, 1)
            for c in range(C):
                last = pe.matmul(bank[7][:, 0:T], ones[:], sq[:, c, :], start=(c == 0), stop=(c == C - 1))
            last.then_inc(ln_var, 1)
            scores(1)
            pe.wait_ge(silu_ready, 1)
            for q in range(4):
                project(CONV0 + q, cen)
                attend(q)
                if q < 2:
                    scores(q + 2)
            pe.wait_ge(ot_out, 4)
            for i in range(NO):
                project(ATTN0 + i, oT)
            for i in range(NW):
                arrived(pe, WOUT0 + i)
                pe.wait_ge(mixed_ready, i + 1)
                for k in range(KPP):
                    for t in range(TT):
                        for h in range(2):
                            last = pe.matmul(bank[3 + 2 * t + h][:], gates[:, 2 * i + k, t * P:(t + 1) * P],
                                             by_rows(WOUT0 + i)[:, k, h * 512:(h + 1) * 512],
                                             start=(i == 0 and k == 0), stop=(i == NW - 1 and k == KPP - 1))
                last.then_inc(piece_done, 1)

            pe.wait_ge(xh_ready, 2 * TT)
            transpose_x((0, 1, 2, 7), hfT_done)
            pe.wait_ge(hfT_ready, 4)
            for t in range(TT):
                for c in range(C):
                    last = pe.matmul(bank[3][:, t * NE:(t + 1) * NE], hfT[:, c, t * P:(t + 1) * P], wrt[:, c, :],
                                     start=(c == 0), stop=(c == C - 1))
            last.then_inc(logit_done, 1)
            pe.wait_ge(member_ready, 1)
            pe.matmul(bank[4][:, 0:NE], before[:], member_h[:, 0, :], start=True, stop=True)
            pe.matmul(bank[4][:, NE:2 * NE], ones_h[:], member_h[:, 0, :], start=True, stop=False)
            pe.matmul(bank[4][:, NE:2 * NE], before[:], member_h[:, 1, :], start=False, stop=True)
            pe.matmul(bank[4][:, 2 * NE:3 * NE], ones_h[:], member_h[:, 0, :], start=True, stop=False)
            pe.matmul(bank[4][:, 2 * NE:3 * NE], ones_h[:], member_h[:, 1, :], start=False, stop=True).then_inc(rank_done, 1)

            def gather(k):
                pe.wait_ge(sel_ready, k + 1)
                for t in range(TT):
                    for h in range(2):
                        last = pe.matmul(G[h * CAP:(h + 1) * CAP, :], sel[:, t, :], xh[:, t, h * 512:(h + 1) * 512],
                                         start=(t == 0), stop=(t == TT - 1))
                last.then_inc(gathered, 1)

            def tokensT(k):
                pe.wait_ge(xg_out, k + 1)
                for i in range(4):
                    last = pe.transpose(G[:, i * P:(i + 1) * P], xg[:, i * P:(i + 1) * P], ident[:])
                last.then_inc(xT_done, 1)

            def scatter(ends):
                for t in range(TT):
                    for h in range(2):
                        rows = slice(h * CAP, (h + 1) * CAP)
                        last = pe.matmul(Y[t][h][:], swT[rows, t, :], yb[rows, :], start=False, stop=ends)
                return last

            def product(dst, first, b, lhs, bias):
                if bias is not None:
                    for h in range(2):
                        pe.matmul(dst[h * CAP:(h + 1) * CAP, :], bsel[0:NE, :], bias[0:NE, h * 512:(h + 1) * 512],
                                  start=True, stop=False)
                for i in range(NW):
                    n = FRONT + first + i
                    arrived(pe, n, b)
                    for k in range(KPP):
                        for h in range(2):
                            last = pe.matmul(dst[h * CAP:(h + 1) * CAP, :], lhs(KPP * i + k),
                                             by_rows(n)[:, k, h * 512:(h + 1) * 512],
                                             start=(bias is None and i == 0 and k == 0), stop=(i == NW - 1 and k == KPP - 1))
                    last.then_inc(piece_done, 1)

            def moe_block(b, off):
                pe.wait_ge(xT_ready, b + (off + 1))
                product(A, 0, b, lambda c: xT[:, c % 4, c // 4, :], bgate)
                pe.wait_ge(swT_out, b + 1)
                product(B, NW, b, lambda c: xT[:, c % 4, c // 4, :], bup)
                gather(b + (off + 1))
                pe.wait_ge(yb_out, b + 1)
                scatter(False)
                pe.wait_ge(act_ready, b + 1)
                for i in range(4):
                    last = pe.transpose(A[:, i * P:(i + 1) * P], hidden[:, i * P:(i + 1) * P], ident[:])
                last.then_inc(actT_done, 1)
                tokensT(b + (off + 1))
                pe.wait_ge(selw_ready, b + 1)
                for t in range(TT):
                    last = pe.transpose(B[:, t * P:(t + 1) * P], selw[:, t, :], ident[:])
                last.then_inc(swT_done, 1)
                pe.wait_ge(actT_out, b + 1)
                product(DN, 2 * NW, b, lambda c: actT[:, c % 4, c // 4, :], None)

            pe.wait_ge(rtr_ready, 1)
            gather(0)
            for t in range(TT):
                last = pe.transpose(bank[5][0:NE, t * P:(t + 1) * P], wts[:, t, 0:NE], ident[:])
            last.then_inc(swT_done, 1)
            tokensT(0)
            pe.wait_ge(wT_out, 1)
            pe.wait_ge(moe_loaded, 64)
            for t in range(TT):
                for h in range(2):
                    pe.matmul(Y[t][h][:], wT[:, t * P:(t + 1) * P], bdown[0:NE, h * 512:(h + 1) * 512], start=True, stop=False)
            with pe.Fori(0, NE) as b:
                moe_block(b, 0)
            pe.wait_ge(n_ready, 1)
            n_blocks = pe.value_load(nblk_i[0:1, 0:1], min_val=NE, max_val=NBLK)
            with pe.If(NE < n_blocks):
                gather(NE + 1)
                tokensT(NE + 1)
            with pe.Fori(NE, NBLK) as b:
                with pe.If(b < n_blocks):
                    moe_block(b, 1)
            pe.wait_ge(yb_out, n_blocks + 1)
            pe.wait_ge(swT_out, n_blocks + 1)
            scatter(True).then_inc(y_done, 1)



_ORDER = ["x", "g_mix", "w_in", "b_in", "conv_w", "conv_b", "conv_ln_g", "conv_ln_b", "w_conv_out", "b_conv_out",
          "attn_sinks", "w_attn_out", "b_attn_out", "w_out", "g_ffn", "w_router", "b_router", "w_gate", "b_gate",
          "w_up", "b_up", "w_down", "b_down", "g_final"]


def kernel(**inputs):
    import numpy as np
    import concourse.bacc as bacc
    from concourse.bass_utils import run_bass_kernel_spmd

    nc = bacc.Bacc("TRN2", target_bir_lowering=False, num_devices=1)
    arrays, aps = {}, {}
    for name in _ORDER:
        a = np.ascontiguousarray(inputs[name])
        arrays[f"in_{name}"] = a
        aps[name] = nc.dram_tensor(f"in_{name}", a.shape, mybir.dt.from_np(a.dtype), kind="ExternalInput").ap()
    out = nc.dram_tensor("out_y", (1, T, D), mybir.dt.float32, kind="ExternalOutput").ap()
    build(nc, aps, out)
    r = run_bass_kernel_spmd(nc, [arrays], core_ids=[0])
    return r.results[0]["out_y"]
```

```python
import concourse.bass as bass
from concourse import mybir
from contextlib import ExitStack

P = 128
D = 1024
T = 256
TT = T // P
C = D // P
KTAPS = 31
HD = 64
NH = 16
GROUP = 8
NE = 32
TOPK = 4
CAP = 64
EPS = 1e-5
LIMIT = 7.0
ALPHA = 1.702
SCALE = HD ** -0.5
SLOPES = [2.0 ** (-8.0 * (h + 1) / NH) for h in range(NH)]
NEG = -1e30

EXTRA = T * TOPK // CAP - 1
PASSES = T // CAP
NBLK = NE + EXTRA

SLOTS = 12
PIECE = 2048
COLS = PIECE // C
KPP = PIECE // D
N_GLU, N_Q, N_KV = 2 * D, D, 2 * 2 * HD

GLU_COLS = [off + COLS * i for i in range(D // COLS) for off in (0, D)]
IN_COLS = GLU_COLS + [N_GLU + COLS * i for i in range((N_Q + N_KV + 2 * D) // COLS)]
NZ = len(IN_COLS)
N_GLUP = len(GLU_COLS)
N_QP = N_Q // COLS
KV_PIECE = N_GLUP + N_QP
GATE0 = KV_PIECE + 1
NO = D // COLS
NW = D // (P * KPP)
CONV0 = NZ
ATTN0 = NZ + NO
WOUT0 = NZ + 2 * NO
FRONT = WOUT0 + NW
MPE = 3 * NW
MORE = 6
MSLOTS = SLOTS + MORE
CYCLE = 3

VEC = {}
_row = 0
for _name, _n in (("g_mix", D), ("b_in", N_GLU + N_Q + N_KV + 2 * D), ("conv_b", D), ("conv_ln_g", D),
                  ("conv_ln_b", D), ("b_conv_out", D), ("b_attn_out", D), ("g_ffn", D)):
    VEC[_name] = (_row, _n // P)
    _row += _n // P
VROWS = _row


def build(nc, t_in, out):
    f32, bf16, i32 = mybir.dt.float32, mybir.dt.bfloat16, mybir.dt.int32
    ALU = mybir.AluOpType
    ACT = mybir.ActivationFunctionType
    X = mybir.AxisListType.X

    ctx = ExitStack()
    with ctx:
        def sb(name, shape, dt=f32):
            return ctx.enter_context(nc.sbuf_tensor(name, shape, dt))

        def sem(name):
            return ctx.enter_context(nc.semaphore(name))

        ring = sb("ring", [P, SLOTS, PIECE])
        x = sb("x_tok", [P, TT, D])
        xh = sb("x_normed", [P, TT, D])
        hT = sb("hT", [P, C, T])
        u = sb("u_padded", [P, C, KTAPS - 1 + T])
        cv = sb("conv_out", [P, C, T])
        gates = sb("gates", [P, 2 * C, T])
        qT = sb("qT", [P, C, T])
        kdup = sb("kT_both_halves", [P, 2, T])
        vT = sb("vT", [P, T])
        v = sb("v_tok", [P, TT, P])
        attn = sb("attention_work", [P, 9 * 4 * P])
        sc = attn[:, 0:6 * 4 * P].rearrange("p (b j s) -> p b j s", b=2, j=4)
        pt = attn[:, 6 * 4 * P:].rearrange("p (k s) -> p k s", k=3)
        spare = sb("spare_piece", [P, PIECE])
        sigb = sb("glu_sigmoid", [P, 2, 2, T])
        vrows = sb("vector_rows", [VROWS, P])
        vecs = sb("vectors", [P, VROWS])
        rows_d = sb("conv_w_rows_then_biases", [2 * NE, D])
        cwrows = rows_d[0:KTAPS, :]
        cw = sb("conv_wT", [P, C, KTAPS])
        ident = sb("ident", [P, P])
        ones = sb("ones", [P, P])
        ones_h = sb("ones_bf16", [P, P], bf16)
        before = sb("strictly_before", [P, P], bf16)
        ndist = sb("minus_distance", [P, 2 * P])
        iota = sb("slot_iota", [P, 2, CAP])
        sinks = sb("sinks", [P, NH])
        brt = sb("b_router", [P, NE])
        wrt = sb("w_router", [P, C, NE])
        eps = sb("eps", [P, 1])
        ss = sb("sums_of_squares", [P, 3, TT])
        std = sb("stds", [P, 2, TT])
        rstd = sb("rstds", [P, 2, TT])
        smax = sb("softmax_max", [P, 2, 4])
        sneg = sb("softmax_minus_max", [P, 2, 2, 4])
        ssum = sb("softmax_sum", [P, 2, 2, 4])
        ssnk = sb("softmax_sink", [P, 2, 2, 4])
        sinks8 = sb("sinks_over_scale", [P, NH])
        logits = sb("logits", [P, TT, NE])
        m8 = sb("top8", [P, TT, 8])
        quota = sb("router_small", [P, 4, TT])
        member_h = sb("member_bf16", [P, TT, NE], bf16)
        member = sb("member", [P, TT, NE])
        wts = sb("weights", [P, TT, NBLK + 1])
        rank = sb("ranks", [P, TT, NBLK + 1])
        ehot = sb("expert_onehot", [2 * NE, NBLK + 1])
        epart = sb("expert_of_partition", [2 * NE, 1])
        cnt = sb("expert_counts", [P, NE])
        flag = sb("further_blocks", [P, PASSES - 1, NE])
        nblk_f = sb("n_blocks_f", [P, 2])
        nblk_i = sb("n_blocks", [P, 1], i32)
        eid_i = sb("expert_ids", [P, EXTRA], i32)

        def over(t, off, *dims):
            flat = t[:].rearrange("p a b -> p (a b)") if len(t.shape) == 3 else t[:]
            n = 1
            for d in dims:
                n *= d
            ap = flat[:, off:off + n]
            if len(dims) == 2:
                ap = ap.rearrange("p (a b) -> p a b", a=dims[0])
            if len(dims) == 3:
                ap = ap.rearrange("p (a b c) -> p a b c", a=dims[0], b=dims[1])
            return ap

        cen = cv
        sq = over(u, 0, C, T)
        glu_work = sigb[:].rearrange("p a b c -> p (a b c)")
        ln_means, ln_stds, ln_rstds = (glu_work[:, k * T:(k + 1) * T] for k in range(3))
        oT = qT
        hfT = cv
        rt = over(kdup, 0, 6 * TT, NE).rearrange("p (k t) e -> p k t e", k=6)
        wT = vT[0:NE, :]
        more = [spare[:], over(hT, 0, PIECE), over(u, 0, PIECE), attn[:, 0:PIECE], attn[:, PIECE:2 * PIECE],
                over(qT, 0, PIECE)]
        gmin, sig, uclip, hidden = (over(gates, 512 * k, 512) for k in range(4))
        actT, xg, xT, yb = over(gates, 2048, 4, 2, CAP), over(gates, 2560, 512), over(gates, 3072, 4, 2, CAP), over(gates, 3584, 512)
        bdown = over(cv, 0, D)
        sel = over(cv, 1024, TT, CAP)
        selw = over(cv, 1152, TT, 2 * CAP)
        swT = over(cv, 1408, TT, P)
        bsel = over(cv, 1664, CAP)
        bgate, bup = rows_d[0:NE, :], rows_d[NE:2 * NE, :]
        gfin = glu_work
        ysum = xh
        tab = over(gates, 0, EXTRA, (PASSES - 1) * NE)
        tab2 = over(gates, 1536, EXTRA, (PASSES - 1) * NE)
        rel = over(kdup, 0, PASSES - 1, NE)
        pos, blockno, eids, zero96, enum = (over(kdup, 96, 96), over(kdup, 192, EXTRA), over(kdup, 208, EXTRA),
                                            over(kdup, 224, 96), over(kdup, 320, NE))

        bank = [ctx.enter_context(nc.psum_tensor(f"bank{i}", [P, 512], f32)) for i in range(8)]
        Y = [[bank[2 * t + h] for h in range(2)] for t in range(TT)]
        A, B, G, DN = bank[4], bank[5], bank[6], bank[7]

        x_loaded, vecs_loaded, small_loaded, k_swapped = sem("x_loaded"), sem("vecs_loaded"), sem("small_loaded"), sem("k_swapped")
        bgu_loaded, bdown_loaded, gfin_loaded, out_stored = sem("bgu_loaded"), sem("bdown_loaded"), sem("gfin_loaded"), sem("out_stored")
        moe_full = [sem(f"moe_full{i}") for i in range(MSLOTS)]
        further_full = [sem(f"further_full{i}") for i in range(MPE)]
        slot_full = [sem(f"slot_full{i}") for i in range(SLOTS)]
        piece_done = sem("piece_done")
        consts = sem("consts")
        u_zero, u_ready = sem("u_zero"), sem("u_ready")
        squares, squares_dve, stds = sem("squares"), sem("squares_dve"), sem("stds")
        z_out, gates_on = sem("z_out"), sem("gates_on")
        ln_sq, ln_std, ln_sig = sem("ln_sq"), sem("ln_std"), sem("ln_sig")
        exps, pt_out, ot_out = sem("exps"), sem("pt_out"), sem("ot_out")
        vecsT, cwT, xTp = sem("vecsT"), sem("cwT"), sem("xTp")
        vtr, s_done, pt_done, pv_done, ln_mean, ln_var = (sem("vtr"), sem("s_done"), sem("pt_done"), sem("pv_done"),
                                                          sem("ln_mean"), sem("ln_var"))
        hfT_done, logit_done, rank_done = sem("hfT_done"), sem("logit_done"), sem("rank_done")
        dve = sem("dve_step")
        vecs_out, cw_out, xh_ready, hT_ready, v_out = sem("vecs_out"), sem("cw_out"), sem("xh_ready"), sem("hT_ready"), sem("v_out")
        taps = sem("taps")
        s_masked, p_ready = sem("s_masked"), sem("p_ready")
        ln_cen, ln_z, silu_ready = sem("ln_cen"), sem("ln_z"), sem("silu_ready")
        y_out, mixed_ready, xnew_ready = sem("y_out"), sem("mixed_ready"), sem("xnew_ready")
        hfT_ready, le_ready, member_ready, rtr_ready, wT_out = (sem("hfT_ready"), sem("le_ready"), sem("member_ready"),
                                                                sem("rtr_ready"), sem("wT_out"))
        le_exp = sem("le_exp")
        n_ready, ov_ready, ov_step = sem("n_ready"), sem("ov_ready"), sem("ov_step")
        sel_ready, gathered, xg_out, xT_done, xT_ready = sem("sel_ready"), sem("gathered"), sem("xg_out"), sem("xT_done"), sem("xT_ready")
        selw_ready, swT_done, swT_out = sem("selw_ready"), sem("swT_done"), sem("swT_out")
        gmin_ready, sig_ready, act_steps, act_ready = sem("gmin_ready"), sem("sig_ready"), sem("act_steps"), sem("act_ready")
        actT_done, actT_out, yb_out = sem("actT_done"), sem("actT_out"), sem("yb_out")
        y_done, ysum_ready = sem("y_done"), sem("ysum_ready")

        def vec(name, c, rows=slice(0, P)):
            return vecs[rows, VEC[name][0] + c:VEC[name][0] + c + 1]

        def by_cols(n):
            return ring[:, n % SLOTS, :].rearrange("p (c n) -> p c n", c=C)

        def by_rows(n):
            return ring[:, n % SLOTS, :].rearrange("p (k n) -> p k n", k=KPP)

        def arrived(eng, n, later=0):
            eng.wait_ge(slot_full[n % SLOTS], 16 * (n // SLOTS + 1) + 16 * later)

        def moe_slot(m):
            s = m % MSLOTS
            if s < SLOTS:
                return by_rows(FRONT + s)
            return more[s - SLOTS].rearrange("p (k n) -> p k n", k=KPP)

        def blocks(eng, run):
            for r in range(CYCLE):
                run(r, r, 0)
            with eng.Fori(1, NE // CYCLE) as cycle:
                for r in range(CYCLE):
                    run(cycle * CYCLE + r, r, cycle)
            for r in range(NE % CYCLE):
                run(NE // CYCLE * CYCLE + r, r, NE // CYCLE)

        block = ctx.enter_context(nc.Block())

        @block.sync
        def _(sp):
            sp.dma_start(x[:], t_in["x"].rearrange("a (t p) d -> p (a t) d", p=P)).then_inc(x_loaded, 16)
            sp.wait_ge(vecs_loaded, 16 * (len(VEC) + 1))

            def fetch(n, dst, src):
                if n >= SLOTS:
                    sp.wait_ge(piece_done, n - SLOTS + 1)
                sp.dma_start(dst, src).then_inc(slot_full[n % SLOTS], 16)

            w_in = t_in["w_in"].rearrange("(c p) n -> p c n", p=P)
            for n, col in enumerate(IN_COLS):
                fetch(n, by_cols(n), w_in[:, :, col:col + COLS])
            for first, name in ((CONV0, "w_conv_out"), (ATTN0, "w_attn_out")):
                w = t_in[name].rearrange("(c p) n -> p c n", p=P)
                for i in range(NO):
                    fetch(first + i, by_cols(first + i), w[:, :, COLS * i:COLS * (i + 1)])
            w = t_in["w_out"].rearrange("(i k p) n -> i p k n", p=P, k=KPP)
            for i in range(NW):
                fetch(WOUT0 + i, by_rows(WOUT0 + i), w[i])

            def piece_of(e, j):
                w = t_in[("w_gate", "w_up", "w_down")[j // NW]].rearrange("e (i k p) n -> e i p k n", p=P, k=KPP)
                if isinstance(e, int):
                    return w[e, j % NW]
                return w[bass.ds(e, 1), j % NW].rearrange("a p k n -> p (a k) n")

            def load(m, e, j):
                sp.dma_start(moe_slot(m), piece_of(e, j)).then_inc(moe_full[m % MSLOTS], 16)

            def first_piece(m, free, value):
                sp.wait_ge(free, value)
                load(m, m // MPE, m % MPE)

            load(SLOTS, SLOTS // MPE, SLOTS % MPE)
            first_piece(SLOTS + 1, piece_done, NZ)
            first_piece(SLOTS + 2, silu_ready, 1)
            first_piece(0, piece_done, FRONT - SLOTS + 1)
            first_piece(SLOTS + 3, pt_done, 12)
            first_piece(SLOTS + 4, pv_done, 4)
            for m in range(1, 8):
                first_piece(m, piece_done, FRONT + m - SLOTS + 1)
            first_piece(SLOTS + 5, piece_done, ATTN0 + NO)
            for m in range(8, SLOTS):
                first_piece(m, piece_done, FRONT + m - SLOTS + 1)

            def expert_pieces(b, r, cycle):
                for j in range(MPE):
                    if isinstance(b, int) and b * MPE + j < MSLOTS:
                        continue
                    sp.wait_ge(piece_done, b * MPE + (FRONT + j - MSLOTS + 1))
                    load(r * MPE + j, b, j)

            blocks(sp, expert_pieces)
            sp.wait_ge(n_ready, 1)
            n_blocks = sp.value_load(nblk_i[0:1, 0:1], min_val=NE, max_val=NBLK)
            with sp.If(NE < n_blocks):
                sp.wait_ge(ov_ready, 1)
                sp.wait_ge(piece_done, FRONT + NE * MPE)
                with sp.Fori(NE, NBLK) as b:
                    with sp.If(b < n_blocks):
                        e = sp.value_load(eid_i[0:1, bass.ds(b - NE, 1)], min_val=0, max_val=NE - 1)
                        for j in range(MPE):
                            sp.wait_ge(piece_done, b * MPE + (FRONT + j - MPE + 1))
                            sp.dma_start(moe_slot(j), piece_of(e, j)).then_inc(further_full[j], 16)
            for t in range(TT):
                sp.wait_ge(ysum_ready, t + 1)
                sp.dma_start(out[0, t * P:(t + 1) * P, :], ysum[:, t, :]).then_inc(out_stored, 16)
            sp.wait_ge(out_stored, 16 * TT)

        @block.gpsimd
        def _(pool):
            own = [0]

            def step(ins):
                own[0] += 1
                ins.then_inc(consts, 1)
                pool.wait_ge(consts, own[0])

            step(pool.memset(ident[:], 0.0))
            step(pool.affine_select(out=ident[:], in_=ident[:], compare_op=ALU.not_equal, fill=1.0, base=0,
                                    pattern=[[-1, P]], channel_multiplier=1))
            step(pool.memset(eps[:], EPS))
            assert own[0] == 3
            pool.memset(u[:, :, 0:KTAPS - 1], 0.0).then_inc(u_zero, 1)
            pool.dma_start(sinks[:], t_in["attn_sinks"].partition_broadcast(P)).then_inc(small_loaded, 16)
            pool.dma_start(brt[:], t_in["b_router"].partition_broadcast(P)).then_inc(small_loaded, 16)
            pool.dma_start(wrt[:], t_in["w_router"].rearrange("(c p) e -> p c e", p=P)).then_inc(small_loaded, 16)
            step(pool.memset(ones[:], 1.0))
            step(pool.memset(ones_h[:], 1.0))
            step(pool.memset(before[:], 1.0))
            step(pool.affine_select(out=before[:], in_=before[:], compare_op=ALU.is_gt, fill=0.0, base=0,
                                    pattern=[[1, P]], channel_multiplier=-1))
            step(pool.iota(ndist[:], pattern=[[1, 2 * P]], base=-P, channel_multiplier=-1,
                           allow_small_or_imprecise_dtypes=True))
            step(pool.affine_select(out=ndist[:], in_=ndist[:], compare_op=ALU.is_ge, fill=NEG, base=P,
                                    pattern=[[-1, 2 * P]], channel_multiplier=1))
            step(pool.affine_select(out=ndist[:], in_=ndist[:], compare_op=ALU.is_ge, fill=NEG, base=-1,
                                    pattern=[[1, 2 * P]], channel_multiplier=-1))
            step(pool.iota(iota[:], pattern=[[0, 2], [1, CAP]], base=0, channel_multiplier=0,
                           allow_small_or_imprecise_dtypes=True))
            for rows in (slice(0, NE), slice(NE, 2 * NE)):
                step(pool.iota(epart[rows, :], pattern=[[0, 1]], base=0, channel_multiplier=1,
                               allow_small_or_imprecise_dtypes=True))
            step(pool.memset(rank[:], -1.0))
            step(pool.memset(wts[:], 0.0))
            step(pool.memset(ehot[:], 0.0))
            for rows in (slice(0, NE), slice(NE, 2 * NE)):
                step(pool.affine_select(out=ehot[rows, 0:NE], in_=ehot[rows, 0:NE], compare_op=ALU.not_equal, fill=1.0,
                                        base=0, pattern=[[-1, NE]], channel_multiplier=1))
            pool.wait_ge(u_zero, 1)
            for i in range(N_GLUP // 2):
                pool.wait_ge(z_out, 2 * i + 2)
                pool.tensor_tensor(u[:, 2 * i:2 * i + 2, KTAPS - 1:], u[:, 2 * i:2 * i + 2, KTAPS - 1:],
                                   sigb[:, i % 2], ALU.mult).then_inc(u_ready, 1)
            pool.wait_ge(cwT, 1)
            pool.dma_start(bgate, t_in["b_gate"]).then_inc(bgu_loaded, 16)
            pool.dma_start(bup, t_in["b_up"]).then_inc(bgu_loaded, 16)

        @block.scalar
        def _(act):
            for name, (row, n) in VEC.items():
                act.dma_start(vrows[row:row + n, :], t_in[name].rearrange("(c p) -> c p", p=P)).then_inc(vecs_loaded, 16)
            act.dma_start(cwrows, t_in["conv_w"]).then_inc(vecs_loaded, 16)

            def token_stds(k, junk, data, ready, count):
                act.preload_act_table(ACT.Sqrt)
                act.wait_ge(ready, count)
                act.activation(junk[:, 0, :], data[:, 0, :], ACT.Square, accum_out=ss[:, k, 0:1]).then_inc(squares, 1)
                act.wait_ge(squares, k + 1)
                act.wait_ge(squares_dve, k + 1)
                act.activation(std[:, k % 2, :], ss[:, k, :], ACT.Sqrt, scale=1.0 / D, bias=eps[:, 0:1]).then_inc(stds, 1)

            act.wait_ge(consts, 3)
            token_stds(0, xh, x, x_loaded, 16)

            act.wait_ge(vecs_out, 1)

            def evacuate(n, dst, func=ACT.Identity):
                act.wait_ge(piece_done, n + 1)
                for j in range(2):
                    last = act.activation(dst[j], bank[n % 3][:, j * T:(j + 1) * T], func,
                                          bias=vec("b_in", IN_COLS[n] // P + j))
                return last.then_inc(z_out, 1)

            for i in range(N_GLUP // 2):
                evacuate(2 * i, [u[:, 2 * i + j, KTAPS - 1:] for j in range(2)])
                if i >= 2:
                    act.wait_ge(u_ready, i - 1)
                act.wait_ge(piece_done, 2 * i + 2)
                for j in range(2):
                    last = act.activation(sigb[:, i % 2, j, :], bank[(2 * i + 1) % 3][:, j * T:(j + 1) * T], ACT.Sigmoid,
                                          bias=vec("b_in", IN_COLS[2 * i + 1] // P + j))
                last.then_inc(z_out, 1)
            for i in range(N_QP):
                evacuate(N_GLUP + i, [qT[:, 2 * i + j, :] for j in range(2)])
            act.wait_ge(piece_done, KV_PIECE + 1)
            for g in range(2):
                rows = slice(g * HD, (g + 1) * HD)
                act.activation(kdup[rows, g, :], bank[KV_PIECE % 3][rows, 0:T], ACT.Identity,
                               bias=vec("b_in", IN_COLS[KV_PIECE] // P, rows))
            act.activation(vT[:], bank[KV_PIECE % 3][:, T:2 * T], ACT.Identity,
                           bias=vec("b_in", IN_COLS[KV_PIECE] // P + 1)).then_inc(z_out, 1)
            act.wait_ge(z_out, KV_PIECE + 1)
            for g in range(2):
                act.dma_start(kdup[(1 - g) * HD:(2 - g) * HD, g, :], kdup[g * HD:(g + 1) * HD, g, :]).then_inc(k_swapped, 16)

            def gate_piece(i):
                evacuate(GATE0 + i, [gates[:, 2 * i + j, :] for j in range(2)])

            def transposed_probs(q):
                if q >= 1:
                    act.wait_ge(pv_done, q)
                for k in range(3):
                    act.wait_ge(pt_done, 3 * q + k + 1)
                    act.activation(pt[:, k, :], bank[6 + (3 * q + k) % 2][:], ACT.Copy).then_inc(pt_out, 1)
                act.wait_ge(pv_done, q + 1)
                g, par = q // 2, q % 2
                rows = slice(par * HD, (par + 1) * HD)
                for n in range(TT):
                    last = act.activation(oT[rows, 4 * g:4 * g + 4, n * P:(n + 1) * P],
                                          bank[3 + n][rows, :].rearrange("p (j q) -> p j q", j=4), ACT.Copy)
                last.then_inc(ot_out, 1)

            def exponentials(q):
                act.wait_ge(s_masked, q + 1)
                for j in range(4):
                    for n, (lo, hi) in enumerate(((0, P), (P, 3 * P))):
                        act.activation(sc[:, q % 2, j, lo:hi], sc[:, q % 2, j, lo:hi], ACT.Exp, scale=SCALE,
                                       bias=sneg[:, q % 2, n, j:j + 1], accum_out=ssum[:, q % 2, n, j:j + 1])
                act.activation(ssnk[:, q % 2], ssnk[:, q % 2], ACT.Exp).then_inc(exps, 1)

            for i in range(4):
                gate_piece(i)
            exponentials(0)
            act.wait_ge(ln_cen, 1)
            act.wait_ge(u_ready, N_GLUP // 2)
            act.activation(sq, cen[:], ACT.Square).then_inc(ln_sq, 1)
            exponentials(1)
            gate_piece(4)
            act.wait_ge(ln_var, 1)
            act.activation(ln_stds, bank[7][:, 0:T], ACT.Sqrt, scale=1.0 / D, bias=eps[:, 0:1]).then_inc(ln_std, 1)
            transposed_probs(0)
            gate_piece(5)
            act.wait_ge(ln_z, 1)
            act.activation(sq, cen[:], ACT.Sigmoid).then_inc(ln_sig, 1)
            gate_piece(6)
            transposed_probs(1)
            exponentials(2)
            gate_piece(7)
            transposed_probs(2)
            act.wait_ge(z_out, NZ)
            act.activation(gates[:], gates[:], ACT.Sigmoid).then_inc(gates_on, 1)
            exponentials(3)
            transposed_probs(3)

            token_stds(1, xh, x, xnew_ready, 1)
            act.preload_act_table(ACT.Exp)
            act.wait_ge(le_ready, 1)
            act.activation(rt[:, 4], rt[:, 4], ACT.Exp).then_inc(le_exp, 1)
            act.dma_start(bdown[0:NE, :], t_in["b_down"]).then_inc(bdown_loaded, 16)
            act.dma_start(gfin, t_in["g_final"].partition_broadcast(P)).then_inc(gfin_loaded, 16)

            def copy_xg(k):
                act.wait_ge(gathered, k + 1)
                act.activation(xg, G[:], ACT.Copy).then_inc(xg_out, 1)

            def moe_block(b, off):
                act.wait_ge(gmin_ready, b + 1)
                act.activation(sig, gmin, ACT.Sigmoid, scale=ALPHA).then_inc(sig_ready, 1)
                copy_xg(b + (off + 1))
                act.wait_ge(actT_done, b + 1)
                act.activation(actT, A[:].rearrange("p (k h s) -> p k h s", k=4, h=2), ACT.Copy).then_inc(actT_out, 1)
                act.wait_ge(swT_done, b + 2)
                act.activation(swT, B[:, 0:T].rearrange("p (t s) -> p t s", t=TT), ACT.Copy).then_inc(swT_out, 1)
                act.wait_ge(piece_done, b * MPE + (FRONT + 3 * NW))
                act.activation(yb, DN[:], ACT.Copy).then_inc(yb_out, 1)

            copy_xg(0)
            with act.Fori(0, NE) as b:
                moe_block(b, 0)
            act.wait_ge(n_ready, 1)
            n_blocks = act.value_load(nblk_i[0:1, 0:1], min_val=NE, max_val=NBLK)
            with act.If(NE < n_blocks):
                copy_xg(NE + 1)
                with act.Fori(NE, NBLK) as b:
                    with act.If(b < n_blocks):
                        moe_block(b, 1)
            token_stds(2, xh, x, xnew_ready, TT + 1)

        @block.vector
        def _(dv):
            own = [0]

            def step(ins):
                own[0] += 1
                ins.then_inc(dve, 1)
                dv.wait_ge(dve, own[0])

            def squares_of_second_tile(k):
                dv.scalar_tensor_tensor(xh[:, 1, :], x[:, 1, :], 1.0, x[:, 1, :], ALU.mult, ALU.mult,
                                        accum_out=ss[:, k, 1:2]).then_inc(squares_dve, 1)

            dv.wait_ge(x_loaded, 16)
            squares_of_second_tile(0)
            dv.wait_ge(vecsT, 1)
            dv.tensor_copy(vecs[:], bank[6][:, 0:VROWS]).then_inc(vecs_out, 1)
            dv.wait_ge(vecs_out, 1)
            dv.wait_ge(stds, 1)
            step(dv.reciprocal(rstd[:, 0, :], std[:, 0, :]))
            for t in range(TT):
                dv.tensor_scalar(xh[:, t, :], x[:, t, :], rstd[:, 0, t:t + 1], None, ALU.mult).then_inc(xh_ready, 1)
            g0 = VEC["g_mix"][0]
            for i in range(4):
                dv.wait_ge(xTp, i + 1)
                dv.tensor_tensor(hT[:, 2 * i:2 * i + 2, :], bank[i][:].rearrange("p (c t) -> p c t", c=2),
                                 vecs[:, g0 + 2 * i:g0 + 2 * i + 2].unsqueeze(2).to_broadcast([P, 2, T]),
                                 ALU.mult).then_inc(hT_ready, 1)

            cb = VEC["conv_b"][0]
            dv.wait_ge(cwT, 1)
            dv.tensor_copy(cw[:], bank[7][:, 0:C * KTAPS].rearrange("p (c k) -> p c k", c=C)).then_inc(cw_out, 1)
            dv.wait_ge(small_loaded, 48)
            step(dv.tensor_scalar(sinks8[:], sinks[:], 1.0 / SCALE, None, ALU.mult))
            dv.wait_ge(cw_out, 1)
            with dv.Fori(0, C // 2) as i:
                dv.wait_ge(u_ready, i + 1)
                for k in range(KTAPS):
                    for j in range(2):
                        src = u[:, bass.ds(2 * i + j, 1), k:k + T].rearrange("p a t -> p (a t)")
                        dst = cv[:, bass.ds(2 * i + j, 1), :].rearrange("p a t -> p (a t)")
                        w = cw[:, bass.ds(2 * i + j, 1), k:k + 1].rearrange("p a t -> p (a t)")
                        if k == 0:
                            ins = dv.tensor_scalar(dst, src, w, vecs[:, bass.ds(cb + 2 * i + j, 1)], ALU.mult, ALU.add)
                        else:
                            dv.wait_ge(taps, 2 * KTAPS * i + 2 * k + j - 1)
                            ins = dv.scalar_tensor_tensor(dst, src, w, dst, ALU.mult, ALU.add)
                        ins.then_inc(taps, 1)
            dv.wait_ge(taps, C * KTAPS)

            def mask_and_max(q):
                g, par = q // 2, q % 2
                h0 = g * GROUP + par
                dv.wait_ge(s_done, q + 1)
                if q == 0:
                    dv.wait_ge(consts, 10)
                if q >= 2:
                    dv.wait_ge(pt_done, 3 * (q - 1))
                for j in range(4):
                    slope = SLOPES[h0 + 2 * j] / SCALE
                    dv.scalar_tensor_tensor(sc[:, q % 2, j, 0:P], ndist[:, P:2 * P], slope,
                                            bank[3][:, j * P:(j + 1) * P], ALU.mult, ALU.add)
                    last = dv.scalar_tensor_tensor(sc[:, q % 2, j, P:3 * P], ndist[:], slope,
                                                   bank[4 + j // 2][:, (j % 2) * T:(j % 2 + 1) * T], ALU.mult, ALU.add)
                step(last)
                dv.reduce_max(smax[:, 0, :], sc[:, q % 2, :, 0:P], axis=X)
                step(dv.reduce_max(smax[:, 1, :], sc[:, q % 2, :, P:3 * P], axis=X))
                snk = sinks8[:, h0:h0 + 7:2].unsqueeze(1).to_broadcast([P, 2, 4])
                step(dv.tensor_tensor(smax[:], smax[:], snk, ALU.max))
                step(dv.tensor_scalar(sneg[:, q % 2], smax[:], -SCALE, None, ALU.mult))
                snk = sinks[:, h0:h0 + 7:2].unsqueeze(1).to_broadcast([P, 2, 4])
                dv.tensor_tensor(ssnk[:, q % 2], sneg[:, q % 2], snk, ALU.add).then_inc(s_masked, 1)

            def divide(q):
                dv.wait_ge(exps, q + 1)
                step(dv.tensor_tensor(ssum[:, q % 2], ssum[:, q % 2], ssnk[:, q % 2], ALU.add))
                step(dv.reciprocal(ssum[:, q % 2], ssum[:, q % 2]))
                for n, (lo, hi) in enumerate(((0, P), (P, 3 * P))):
                    last = dv.tensor_tensor(sc[:, q % 2, :, lo:hi], sc[:, q % 2, :, lo:hi],
                                            ssum[:, q % 2, n, :].unsqueeze(2).to_broadcast([P, 4, hi - lo]), ALU.mult)
                last.then_inc(p_ready, 1)

            def out_piece(k, i):
                n = (CONV0, ATTN0)[k] + i
                dv.wait_ge(piece_done, n + 1)
                dv.wait_ge(gates_on, 1)
                for j in range(2):
                    c = 2 * i + j
                    last = dv.scalar_tensor_tensor(gates[:, k * C + c, :], bank[n % 3][:, j * T:(j + 1) * T],
                                                   vec(("b_conv_out", "b_attn_out")[k], c), gates[:, k * C + c, :],
                                                   ALU.add, ALU.mult)
                last.then_inc(y_out, 1)

            def further_blocks():
                NP = PASSES - 1
                own = [0]

                def step(ins):
                    own[0] += 1
                    ins.then_inc(ov_step, 1)
                    dv.wait_ge(ov_step, own[0])

                dv.wait_ge(yb_out, NE)
                dv.memset(zero96, 0.0)
                for i in range(EXTRA):
                    dv.memset(blockno[:, i:i + 1], float(i + 1))
                for e in range(NE):
                    last = dv.memset(enum[:, e:e + 1], float(e))
                step(last)
                ff = flag[:].rearrange("p a b -> p (a b)")
                step(dv.tensor_tensor_scan(pos, ff, zero96, 0.0, ALU.add, ALU.add))
                step(dv.tensor_tensor(tab, pos.unsqueeze(1).to_broadcast([P, EXTRA, NP * NE]),
                                      blockno.unsqueeze(2).to_broadcast([P, EXTRA, NP * NE]), ALU.is_equal))
                step(dv.tensor_tensor(tab, tab, ff.unsqueeze(1).to_broadcast([P, EXTRA, NP * NE]), ALU.mult))

                def picked(dst, values):
                    step(dv.tensor_tensor(tab2, tab, values.unsqueeze(1).to_broadcast([P, EXTRA, NP * NE]), ALU.mult))
                    step(dv.reduce_sum(dst, tab2, axis=X))

                relf = rel.rearrange("p a b -> p (a b)")
                for t in range(TT):
                    for k in range(NP):
                        last = dv.tensor_scalar(rel[:, k, :], rank[:, t, 0:NE], -float(CAP * (k + 1)), None, ALU.add)
                    step(last)
                    picked(rank[:, t, NE:NBLK], relf)
                    for k in range(NP):
                        last = dv.tensor_copy(rel[:, k, :], wts[:, t, 0:NE])
                    step(last)
                    picked(wts[:, t, NE:NBLK], relf)
                for k in range(NP):
                    last = dv.tensor_copy(rel[:, k, :], enum)
                step(last)
                picked(eids, relf)
                step(dv.tensor_scalar(ehot[:, NE:NBLK], eids[0:2 * NE, :], epart[:, 0:1], None, ALU.is_equal))
                dv.tensor_copy(eid_i[:], eids).then_inc(ov_ready, 1)

            dv.wait_ge(vtr, 1)
            dv.tensor_copy(v[:], bank[6][:, 0:T].rearrange("p (t c) -> p t c", t=TT)).then_inc(v_out, 1)
            mask_and_max(0)
            dv.wait_ge(ln_mean, 1)
            step(dv.tensor_scalar(ln_means, bank[7][:, 0:T], 1.0 / D, None, ALU.mult))
            dv.tensor_tensor(cen[:], cv[:], ln_means.unsqueeze(1).to_broadcast([P, C, T]), ALU.subtract).then_inc(ln_cen, 1)
            divide(0)
            mask_and_max(1)
            dv.wait_ge(ln_std, 1)
            step(dv.reciprocal(ln_rstds, ln_stds))
            step(dv.tensor_tensor(cen[:], cen[:], ln_rstds.unsqueeze(1).to_broadcast([P, C, T]), ALU.mult))
            for c in range(C):
                last = dv.tensor_scalar(cen[:, c, :], cen[:, c, :], vec("conv_ln_g", c), vec("conv_ln_b", c), ALU.mult, ALU.add)
            last.then_inc(ln_z, 1)
            divide(1)
            dv.wait_ge(ln_sig, 1)
            dv.tensor_tensor(cen[:], cen[:], sq, ALU.mult).then_inc(silu_ready, 1)
            mask_and_max(2)
            divide(2)
            mask_and_max(3)
            out_piece(0, 0)
            divide(3)
            for i in range(1, NO):
                out_piece(0, i)
            for i in range(NO):
                out_piece(1, i)
                dv.wait_ge(y_out, NO + i + 1)
                dv.tensor_tensor(gates[:, 2 * i:2 * i + 2, :], gates[:, 2 * i:2 * i + 2, :],
                                 gates[:, C + 2 * i:C + 2 * i + 2, :], ALU.add).then_inc(mixed_ready, 1)

            dv.wait_ge(piece_done, FRONT)
            for t in range(TT):
                for h in range(2):
                    last = dv.tensor_tensor(x[:, t, h * 512:(h + 1) * 512], x[:, t, h * 512:(h + 1) * 512],
                                            bank[3 + 2 * t + h][:], ALU.add)
                last.then_inc(xnew_ready, 1)
            dv.wait_ge(xnew_ready, 2)
            squares_of_second_tile(1)
            dv.wait_ge(stds, 2)
            step(dv.reciprocal(rstd[:, 1, :], std[:, 1, :]))
            for t in range(TT):
                dv.tensor_scalar(xh[:, t, :], x[:, t, :], rstd[:, 1, t:t + 1], None, ALU.mult).then_inc(xh_ready, 1)
            g1 = VEC["g_ffn"][0]
            for i in range(4):
                dv.wait_ge(hfT_done, i + 1)
                dv.tensor_tensor(hfT[:, 2 * i:2 * i + 2, :], bank[(0, 1, 2, 7)[i]][:].rearrange("p (c t) -> p c t", c=2),
                                 vecs[:, g1 + 2 * i:g1 + 2 * i + 2].unsqueeze(2).to_broadcast([P, 2, T]),
                                 ALU.mult).then_inc(hfT_ready, 1)

            L, gt, eq, cum, le, tmp = logits[:], rt[:, 0], rt[:, 1], rt[:, 2], rt[:, 4], rt[:, 5]
            dv.wait_ge(logit_done, 1)
            step(dv.tensor_tensor(L, bank[3][:, 0:TT * NE].rearrange("p (t e) -> p t e", t=TT),
                                  brt[:].unsqueeze(1).to_broadcast([P, TT, NE]), ALU.add))
            dv.max(m8[:, 0, :], L[:, 0, :])
            step(dv.max(m8[:, 1, :], L[:, 1, :]))
            dv.tensor_tensor(le, L, m8[:, :, 0:1].to_broadcast([P, TT, NE]), ALU.subtract).then_inc(le_ready, 1)
            fourth = m8[:, :, TOPK - 1:TOPK].to_broadcast([P, TT, NE])
            dv.tensor_tensor(eq, L, fourth, ALU.is_equal)
            step(dv.tensor_tensor(gt, L, fourth, ALU.is_gt))
            for t in range(TT):
                step(dv.tensor_tensor_scan(cum[:, t, :], eq[:, t, :], eq[:, t, :], 0.0, ALU.add, ALU.max))
            step(dv.reduce_sum(quota[:, 0, :], gt, axis=X))
            step(dv.tensor_tensor(cum, cum, quota[:, 0, :].unsqueeze(2).to_broadcast([P, TT, NE]), ALU.add))
            step(dv.scalar_tensor_tensor(tmp, cum, float(TOPK), eq, ALU.is_le, ALU.mult))
            step(dv.tensor_tensor(member[:], gt, tmp, ALU.add))
            dv.tensor_copy(member_h[:], member[:]).then_inc(member_ready, 1)
            dv.wait_ge(le_exp, 1)
            step(dv.tensor_tensor(le, le, member[:], ALU.mult))
            step(dv.reduce_sum(quota[:, 1, :], le, axis=X))
            step(dv.reciprocal(quota[:, 2, :], quota[:, 1, :]))
            dv.wait_ge(consts, 18)
            step(dv.tensor_tensor(wts[:, :, 0:NE], le, quota[:, 2, :].unsqueeze(2).to_broadcast([P, TT, NE]), ALU.mult))
            dv.wait_ge(rank_done, 1)
            step(dv.scalar_tensor_tensor(tmp, bank[4][:, 0:TT * NE].rearrange("p (t e) -> p t e", t=TT), 1.0, member[:],
                                         ALU.add, ALU.mult))
            step(dv.tensor_scalar(rank[:, :, 0:NE], tmp, -1.0, None, ALU.add))
            dv.tensor_copy(cnt[:], bank[4][:, TT * NE:(TT + 1) * NE]).then_inc(rtr_ready, 1)

            def select(b, k):
                if not isinstance(k, int) or k > 0:
                    dv.wait_ge(gathered, k)
                for t in range(TT):
                    last = dv.tensor_scalar(sel[:, t, :], iota[:, 0, :], rank[:, t, bass.ds(b, 1)], None, ALU.is_equal)
                last.then_inc(sel_ready, 1)

            def tokensT(b, k):
                dv.wait_ge(xT_done, k + 1)
                dv.tensor_scalar(bsel[0:2 * NE, :], ones[0:2 * NE, 0:CAP], ehot[:, bass.ds(b, 1)], None, ALU.mult)
                ge = vecs[:, g1:g1 + C].rearrange("p (h k) -> p k h", h=2).unsqueeze(3).to_broadcast([P, 4, 2, CAP])
                dv.tensor_tensor(xT, G[:].rearrange("p (k h s) -> p k h s", k=4, h=2), ge, ALU.mult).then_inc(xT_ready, 1)

            def moe_block(b, off):
                select(b + 1, b + (off + 1))
                dv.wait_ge(swT_done, b + 1)
                for t in range(TT):
                    last = dv.tensor_scalar(selw[:, t, :], iota[:].rearrange("p a s -> p (a s)"), rank[:, t, bass.ds(b, 1)],
                                            wts[:, t, bass.ds(b, 1)], ALU.is_equal, ALU.mult)
                last.then_inc(selw_ready, 1)
                dv.wait_ge(piece_done, b * MPE + (FRONT + NW))
                dv.tensor_scalar(gmin, A[:], LIMIT, None, ALU.min).then_inc(gmin_ready, 1)
                dv.wait_ge(sig_ready, b + 1)
                dv.tensor_tensor(gmin, gmin, sig, ALU.mult).then_inc(act_steps, 1)
                dv.wait_ge(piece_done, b * MPE + (FRONT + 2 * NW))
                dv.tensor_scalar(uclip, B[:], LIMIT, -LIMIT, ALU.min, ALU.max).then_inc(act_steps, 1)
                dv.wait_ge(act_steps, 2 * b + 2)
                dv.scalar_tensor_tensor(hidden, uclip, 1.0, gmin, ALU.add, ALU.mult).then_inc(act_ready, 1)
                tokensT(b + 1, b + (off + 1))

            select(0, 0)
            dv.wait_ge(rtr_ready, 1)
            for k in range(1, PASSES):
                last = dv.tensor_scalar(flag[:, k - 1, :], cnt[:], float(CAP * k), None, ALU.is_gt)
            step(last)
            step(dv.reduce_sum(nblk_f[:, 0:1], flag[:].rearrange("p a b -> p (a b)"), axis=X))
            dv.tensor_scalar(nblk_i[:], nblk_f[:, 0:1], float(NE), None, ALU.add).then_inc(n_ready, 1)
            tokensT(0, 0)
            dv.wait_ge(swT_done, 1)
            dv.tensor_copy(wT, bank[5][0:NE, 0:T]).then_inc(wT_out, 1)
            with dv.Fori(0, NE) as b:
                moe_block(b, 0)

            n_blocks = dv.value_load(nblk_i[0:1, 0:1], min_val=NE, max_val=NBLK)
            with dv.If(NE < n_blocks):
                further_blocks()
                select(NE, NE + 1)
                tokensT(NE, NE + 1)
                with dv.Fori(NE, NBLK) as b:
                    with dv.If(b < n_blocks):
                        moe_block(b, 1)

            for t in range(TT):
                dv.wait_ge(y_done, t + 1)
                for h in range(2):
                    last = dv.tensor_tensor(x[:, t, h * 512:(h + 1) * 512], x[:, t, h * 512:(h + 1) * 512], Y[t][h][:], ALU.add)
                last.then_inc(xnew_ready, 1)
            dv.wait_ge(xnew_ready, 2 * TT)
            dv.wait_ge(gfin_loaded, 16)
            squares_of_second_tile(2)
            dv.wait_ge(stds, 3)
            dv.reciprocal(rstd[:, 0, :], std[:, 0, :]).then_inc(vecs_out, 1)
            dv.wait_ge(vecs_out, 2)
            for t in range(TT):
                dv.scalar_tensor_tensor(ysum[:, t, :], x[:, t, :], rstd[:, 0, t:t + 1], gfin, ALU.mult, ALU.mult).then_inc(ysum_ready, 1)


        @block.tensor
        def _(pe):
            pe.wait_ge(consts, 2)
            pe.wait_ge(vecs_loaded, 16 * (len(VEC) + 1))
            pe.transpose(bank[6][:, 0:VROWS], vrows[:], ident[0:VROWS, 0:VROWS]).then_inc(vecsT, 1)
            for c in range(C):
                last = pe.transpose(bank[7][:, c * KTAPS:(c + 1) * KTAPS], cwrows[:, c * P:(c + 1) * P],
                                    ident[0:KTAPS, 0:KTAPS])
            last.then_inc(cwT, 1)

            def transpose_x(banks, done):
                for i in range(4):
                    for j in range(2):
                        for t in range(TT):
                            c = 2 * i + j
                            last = pe.transpose(bank[banks[i]][:, j * T + t * P:j * T + (t + 1) * P],
                                                xh[:, t, c * P:(c + 1) * P], ident[:])
                    last.then_inc(done, 1)

            pe.wait_ge(xh_ready, TT)
            transpose_x((0, 1, 2, 3), xTp)
            pe.wait_ge(hT_ready, 4)

            def project(n, src):
                arrived(pe, n)
                if n >= 3:
                    m = n - 3
                    if m < NZ:
                        pe.wait_ge(z_out, m + 1)
                    else:
                        pe.wait_ge(y_out, m - NZ + 1)
                w = by_cols(n)
                for j in range(2):
                    for c in range(C):
                        last = pe.matmul(bank[n % 3][:, j * T:(j + 1) * T], w[:, c, j * P:(j + 1) * P], src[:, c, :],
                                         start=(c == 0), stop=(c == C - 1))
                last.then_inc(piece_done, 1)

            def scores(q):
                g, par = q // 2, q % 2
                rows = slice(par * HD, (par + 1) * HD)
                if q == 0:
                    pe.wait_ge(k_swapped, 32)
                else:
                    pe.wait_ge(s_masked, q)
                if q >= 2:
                    pe.wait_ge(ot_out, q - 1)
                for j in range(4):
                    pe.matmul(bank[3][:, j * P:(j + 1) * P], qT[rows, 4 * g + j, 0:P], kdup[rows, g, 0:P],
                              start=True, stop=True)
                for j in range(4):
                    last = pe.matmul(bank[4 + j // 2][:, (j % 2) * T:(j % 2 + 1) * T], qT[rows, 4 * g + j, P:T],
                                     kdup[rows, g, :], start=True, stop=True)
                last.then_inc(s_done, 1)

            def attend(q):
                g, par = q // 2, q % 2
                rows = slice(par * HD, (par + 1) * HD)
                pe.wait_ge(p_ready, q + 1)
                for k in range(3):
                    if 3 * q + k >= 2:
                        pe.wait_ge(pt_out, 3 * q + k - 1)
                    for j in range(4):
                        last = pe.transpose(bank[6 + (3 * q + k) % 2][:, j * P:(j + 1) * P],
                                            sc[:, q % 2, j, k * P:(k + 1) * P], ident[:])
                    last.then_inc(pt_done, 1)
                if q < 3:
                    pe.wait_ge(s_masked, q + 2)
                pe.wait_ge(pt_out, 3 * q + 3)
                kv = slice(g * HD, (g + 1) * HD)
                pe.matmul(bank[3][rows, :], v[:, 0, kv], pt[:, 0, :], start=True, stop=True)
                pe.matmul(bank[4][rows, :], v[:, 0, kv], pt[:, 1, :], start=True, stop=False)
                pe.matmul(bank[4][rows, :], v[:, 1, kv], pt[:, 2, :], start=False, stop=True).then_inc(pv_done, 1)

            for n in range(GATE0):
                project(n, hT)
            pe.wait_ge(z_out, GATE0)
            pe.wait_ge(cw_out, 1)
            for t in range(TT):
                last = pe.transpose(bank[6][:, t * P:(t + 1) * P], vT[:, t * P:(t + 1) * P], ident[:])
            last.then_inc(vtr, 1)
            scores(0)
            for i in range(4):
                project(GATE0 + i, hT)
            pe.wait_ge(taps, C * KTAPS)
            for c in range(C):
                last = pe.matmul(bank[7][:, 0:T], ones[:], cv[:, c, :], start=(c == 0), stop=(c == C - 1))
            last.then_inc(ln_mean, 1)
            scores(1)
            project(GATE0 + 4, hT)
            pe.wait_ge(ln_sq, 1)
            for c in range(C):
                last = pe.matmul(bank[7][:, 0:T], ones[:], sq[:, c, :], start=(c == 0), stop=(c == C - 1))
            last.then_inc(ln_var, 1)
            pe.wait_ge(v_out, 1)
            pe.wait_ge(ln_std, 1)
            attend(0)
            scores(2)
            project(GATE0 + 5, hT)
            project(GATE0 + 6, hT)
            attend(1)
            scores(3)
            project(GATE0 + 7, hT)
            attend(2)
            pe.wait_ge(silu_ready, 1)
            project(CONV0, cen)
            project(CONV0 + 1, cen)
            attend(3)
            project(CONV0 + 2, cen)
            project(CONV0 + 3, cen)
            pe.wait_ge(ot_out, 4)
            for i in range(NO):
                project(ATTN0 + i, oT)
            for i in range(NW):
                arrived(pe, WOUT0 + i)
                pe.wait_ge(mixed_ready, i + 1)
                for k in range(KPP):
                    for t in range(TT):
                        for h in range(2):
                            last = pe.matmul(bank[3 + 2 * t + h][:], gates[:, 2 * i + k, t * P:(t + 1) * P],
                                             by_rows(WOUT0 + i)[:, k, h * 512:(h + 1) * 512],
                                             start=(i == 0 and k == 0), stop=(i == NW - 1 and k == KPP - 1))
                last.then_inc(piece_done, 1)

            pe.wait_ge(xh_ready, 2 * TT)
            transpose_x((0, 1, 2, 7), hfT_done)
            pe.wait_ge(hfT_ready, 4)
            for t in range(TT):
                for c in range(C):
                    last = pe.matmul(bank[3][:, t * NE:(t + 1) * NE], hfT[:, c, t * P:(t + 1) * P], wrt[:, c, :],
                                     start=(c == 0), stop=(c == C - 1))
            last.then_inc(logit_done, 1)
            pe.wait_ge(member_ready, 1)
            pe.matmul(bank[4][:, 0:NE], before[:], member_h[:, 0, :], start=True, stop=True)
            pe.matmul(bank[4][:, NE:2 * NE], ones_h[:], member_h[:, 0, :], start=True, stop=False)
            pe.matmul(bank[4][:, NE:2 * NE], before[:], member_h[:, 1, :], start=False, stop=True)
            pe.matmul(bank[4][:, 2 * NE:3 * NE], ones_h[:], member_h[:, 0, :], start=True, stop=False)
            pe.matmul(bank[4][:, 2 * NE:3 * NE], ones_h[:], member_h[:, 1, :], start=False, stop=True).then_inc(rank_done, 1)

            def gather(k):
                pe.wait_ge(sel_ready, k + 1)
                for t in range(TT):
                    for h in range(2):
                        last = pe.matmul(G[h * CAP:(h + 1) * CAP, :], sel[:, t, :], xh[:, t, h * 512:(h + 1) * 512],
                                         start=(t == 0), stop=(t == TT - 1))
                last.then_inc(gathered, 1)

            def tokensT(k):
                pe.wait_ge(xg_out, k + 1)
                for i in range(4):
                    last = pe.transpose(G[:, i * P:(i + 1) * P], xg[:, i * P:(i + 1) * P], ident[:])
                last.then_inc(xT_done, 1)

            def scatter(ends=False):
                for t in range(TT):
                    for h in range(2):
                        rows = slice(h * CAP, (h + 1) * CAP)
                        last = pe.matmul(Y[t][h][:], swT[rows, t, :], yb[rows, :], start=False, stop=ends)
                    if ends:
                        last.then_inc(y_done, 1)

            def product(dst, first, piece, lhs, bias):
                if bias is not None:
                    rows = slice(0, NE) if bias is bgate else slice(NE, 2 * NE)
                    for h in range(2):
                        pe.matmul(dst[h * CAP:(h + 1) * CAP, :], bsel[rows, :], bias[:, h * 512:(h + 1) * 512],
                                  start=True, stop=False)
                for i in range(NW):
                    j = first + i
                    w = piece(j)
                    for k in range(KPP):
                        for h in range(2):
                            last = pe.matmul(dst[h * CAP:(h + 1) * CAP, :], lhs(KPP * i + k), w[:, k, h * 512:(h + 1) * 512],
                                             start=(bias is None and i == 0 and k == 0), stop=(i == NW - 1 and k == KPP - 1))
                    last.then_inc(piece_done, 1)

            def start_y():
                pe.wait_ge(wT_out, 1)
                pe.wait_ge(bdown_loaded, 16)
                for t in range(TT):
                    for h in range(2):
                        pe.matmul(Y[t][h][:], wT[:, t * P:(t + 1) * P], bdown[0:NE, h * 512:(h + 1) * 512], start=True, stop=False)

            def piece_of_cycle(r, cycle):
                def piece(j):
                    m = r * MPE + j
                    pe.wait_ge(moe_full[m % MSLOTS], cycle * (16 * CYCLE * MPE // MSLOTS) + 16 * (m // MSLOTS + 1))
                    return moe_slot(m)
                return piece

            def piece_of_further(i):
                def piece(j):
                    pe.wait_ge(further_full[j], i * 16 + 16)
                    return moe_slot(j)
                return piece

            def moe_block(b, off, piece):
                first = isinstance(b, int) and b == 0
                pe.wait_ge(xT_ready, b + (off + 1))
                product(A, 0, piece, lambda c: xT[:, c % 4, c // 4, :], bgate)
                if first:
                    pe.wait_ge(wT_out, 1)
                else:
                    pe.wait_ge(swT_out, b)
                product(B, NW, piece, lambda c: xT[:, c % 4, c // 4, :], bup)
                gather(b + (off + 1))
                if first:
                    start_y()
                else:
                    pe.wait_ge(yb_out, b)
                    scatter()
                pe.wait_ge(act_ready, b + 1)
                for i in range(4):
                    last = pe.transpose(A[:, i * P:(i + 1) * P], hidden[:, i * P:(i + 1) * P], ident[:])
                last.then_inc(actT_done, 1)
                tokensT(b + (off + 1))
                pe.wait_ge(selw_ready, b + 1)
                for t in range(TT):
                    last = pe.transpose(B[:, t * P:(t + 1) * P], selw[:, t, :], ident[:])
                last.then_inc(swT_done, 1)
                pe.wait_ge(actT_out, b + 1)
                product(DN, 2 * NW, piece, lambda c: actT[:, c % 4, c // 4, :], None)

            pe.wait_ge(rtr_ready, 1)
            gather(0)
            for t in range(TT):
                last = pe.transpose(bank[5][0:NE, t * P:(t + 1) * P], wts[:, t, 0:NE], ident[:])
            last.then_inc(swT_done, 1)
            tokensT(0)
            pe.wait_ge(bgu_loaded, 32)
            blocks(pe, lambda b, r, cycle: moe_block(b, 0, piece_of_cycle(r, cycle)))
            pe.wait_ge(n_ready, 1)
            n_blocks = pe.value_load(nblk_i[0:1, 0:1], min_val=NE, max_val=NBLK)
            with pe.If(NE < n_blocks):
                gather(NE + 1)
                tokensT(NE + 1)
                with pe.Fori(NE, NBLK) as b:
                    with pe.If(b < n_blocks):
                        moe_block(b, 1, piece_of_further(b - NE))
            pe.wait_ge(yb_out, n_blocks)
            pe.wait_ge(swT_out, n_blocks)
            scatter(True)



_ORDER = ["x", "g_mix", "w_in", "b_in", "conv_w", "conv_b", "conv_ln_g", "conv_ln_b", "w_conv_out", "b_conv_out",
          "attn_sinks", "w_attn_out", "b_attn_out", "w_out", "g_ffn", "w_router", "b_router", "w_gate", "b_gate",
          "w_up", "b_up", "w_down", "b_down", "g_final"]


def kernel(**inputs):
    import numpy as np
    import concourse.bacc as bacc
    from concourse.bass_utils import run_bass_kernel_spmd

    nc = bacc.Bacc("TRN2", target_bir_lowering=False, num_devices=1)
    arrays, aps = {}, {}
    for name in _ORDER:
        a = np.ascontiguousarray(inputs[name])
        arrays[f"in_{name}"] = a
        aps[name] = nc.dram_tensor(f"in_{name}", a.shape, mybir.dt.from_np(a.dtype), kind="ExternalInput").ap()
    out = nc.dram_tensor("out_y", (1, T, D), mybir.dt.float32, kind="ExternalOutput").ap()
    build(nc, aps, out)
    r = run_bass_kernel_spmd(nc, [arrays], core_ids=[0])
    return r.results[0]["out_y"]
```

```python
import concourse.bass as bass
from concourse import mybir
from contextlib import ExitStack

P = 128
D = 1024
T = 256
TT = T // P
C = D // P
KTAPS = 31
HD = 64
NH = 16
NE = 32
TOPK = 4
CAP = 64
EPS = 1e-5
LIMIT = 7.0
ALPHA = 1.702
SCALE = HD ** -0.5
SLOPES = [2.0 ** (-8.0 * (h + 1) / NH) for h in range(NH)]
NEG = -1e30

EXTRA = T * TOPK // CAP - 1
PASSES = T // CAP
NBLK = NE + EXTRA

SLOTS = 12
PIECE = 2048
COLS = PIECE // C
KPP = PIECE // D
N_GLU, N_Q, N_KV = 2 * D, D, 2 * 2 * HD

GLU_COLS = [off + COLS * i for i in range(D // COLS) for off in (0, D)]
IN_COLS = GLU_COLS + [N_GLU + COLS * i for i in range((N_Q + N_KV + 2 * D) // COLS)]
NZ = len(IN_COLS)
N_GLUP = len(GLU_COLS)
N_QP = N_Q // COLS
KV_PIECE = N_GLUP + N_QP
GATE0 = KV_PIECE + 1
NO = D // COLS
NW = D // (P * KPP)
CONV0 = NZ
ATTN0 = NZ + NO
WOUT0 = NZ + 2 * NO
FRONT = WOUT0 + NW
MPE = 3 * NW
MORE = 8
MSLOTS = SLOTS + MORE
CYCLE = 5

assert CYCLE * MPE % MSLOTS == 0

VEC = {}
_row = 0
for _name, _n in (("g_mix", D), ("b_in", N_GLU + N_Q + N_KV + 2 * D), ("conv_b", D), ("conv_ln_g", D),
                  ("conv_ln_b", D), ("b_conv_out", D), ("b_attn_out", D), ("g_ffn", D)):
    VEC[_name] = (_row, _n // P)
    _row += _n // P
VROWS = _row


def build(nc, t_in, out):
    f32, bf16, i32 = mybir.dt.float32, mybir.dt.bfloat16, mybir.dt.int32
    ALU = mybir.AluOpType
    ACT = mybir.ActivationFunctionType
    X = mybir.AxisListType.X

    ctx = ExitStack()
    with ctx:
        def sb(name, shape, dt=f32):
            return ctx.enter_context(nc.sbuf_tensor(name, shape, dt))

        def sem(name):
            return ctx.enter_context(nc.semaphore(name))

        ring = sb("ring", [P, SLOTS, PIECE])
        x = sb("x_tok", [P, TT, D])
        xh = sb("x_normed", [P, TT, D])
        hT = sb("hT", [P, C, T])
        u = sb("u_padded", [P, C, KTAPS - 1 + T])
        cv = sb("conv_out", [P, C, T])
        gates = sb("gates", [P, 2 * C, T])
        qT = sb("qT", [P, C, T])
        kpad = sb("kT_zero_padded", [P, 4, T])
        vT = sb("vT", [P, T])
        v = sb("v_tok", [P, TT, P])
        attn = sb("attention_work", [P, 9 * 4 * P])
        sc = attn[:, 0:6 * 4 * P].rearrange("p (b j s) -> p b j s", b=2, j=4)
        pt = attn[:, 6 * 4 * P:].rearrange("p (k s) -> p k s", k=3)
        vrows = attn[0:VROWS, 0:P]
        cw = attn[:, P:P + C * KTAPS].rearrange("p (c k) -> p c k", c=C)
        spare = sb("spare_piece", [P, PIECE])
        sigb = sb("glu_sigmoid", [P, 2, 2, T])
        vecs = sb("vectors", [P, VROWS])
        rows_d = sb("conv_w_rows_then_biases", [2 * NE, D])
        cwrows = rows_d[0:KTAPS, :]
        ident = sb("ident", [P, P])
        ident4 = sb("four_idents", [P, NE])
        ones = sb("ones", [P, P])
        ones_h = sb("ones_bf16", [P, P], bf16)
        before = sb("strictly_before", [P, P], bf16)
        ndist = sb("minus_distance", [P, 2 * P])
        iota = sb("slot_iota", [P, 2, CAP])
        sinks = sb("sinks", [P, NH])
        brt = sb("b_router", [P, NE])
        wrt = sb("w_router", [P, C, NE])
        eps = sb("eps", [P, 1])
        ss = sb("sums_of_squares", [P, 4, TT])
        std = sb("stds", [P, 2, TT])
        rstd = sb("rstds", [P, 2, TT])
        smax = sb("softmax_max", [P, 2, 4])
        sneg = sb("softmax_minus_max", [P, 2, 2, 4])
        ssum = sb("softmax_sum", [P, 2, 2, 4])
        ssnk = sb("softmax_sink", [P, 2, 2, 4])
        sinks8 = sb("sinks_over_scale", [P, NH])
        m8 = sb("top8", [P, TT, 8])
        quota = sb("router_small", [P, 4, TT])
        member_h = sb("member_bf16", [P, TT, NE], bf16)
        wts = sb("weights", [P, TT, NBLK + 1])
        rank = sb("ranks", [P, TT, NBLK + 1])
        ehot = sb("expert_onehot", [2 * NE, NBLK + 1])
        epart = sb("expert_of_partition", [2 * NE, 1])
        nblk_f = sb("n_blocks_f", [P, 2])
        nblk_i = sb("n_blocks", [P, 1], i32)
        eid_i = sb("expert_ids", [P, EXTRA], i32)

        def over(t, off, *dims):
            flat = t[:].rearrange("p a b -> p (a b)") if len(t.shape) == 3 else t[:]
            n = 1
            for d in dims:
                n *= d
            ap = flat[:, off:off + n]
            if len(dims) == 2:
                ap = ap.rearrange("p (a b) -> p a b", a=dims[0])
            if len(dims) == 3:
                ap = ap.rearrange("p (a b c) -> p a b c", a=dims[0], b=dims[1])
            return ap

        cen = cv
        sq = over(u, 0, C, T)
        glu_work = sigb[:].rearrange("p a b c -> p (a b c)")
        ln_means, ln_stds, ln_rstds, ln_sums = (glu_work[:, k * T:(k + 1) * T] for k in range(4))
        oT = qT
        hfT = cv
        rt = over(kpad, 0, 6 * TT, NE).rearrange("p (k t) e -> p k t e", k=6)
        wT = vT[0:NE, :]
        logits, member, cnt, flag = (over(kpad, 384, TT, NE), over(kpad, 448, TT, NE), over(kpad, 512, NE),
                                     over(kpad, 544, PASSES - 1, NE))
        more = [spare[:], over(hT, 0, PIECE), over(u, 0, PIECE), attn[:, 0:PIECE], attn[:, PIECE:2 * PIECE],
                over(qT, 0, PIECE), over(gates, 0, PIECE), x[:].rearrange("p t d -> p (t d)")]
        xT, actT = over(gates, PIECE, 4, 2, CAP), over(gates, PIECE + 512, 4, 2, CAP)
        yb, xg = over(gates, PIECE + 1024, 512), over(gates, PIECE + 1536, 512)
        sig = xg
        gmin, hidden = over(cv, 0, 512), over(cv, 512, 512)
        uclip = hidden
        sel = over(cv, 1024, TT, CAP)
        selw = over(cv, 1152, TT, 2 * CAP)
        swT = over(cv, 1408, TT, P)
        bsel = over(cv, 1664, CAP)
        bdown = glu_work
        bgate, bup = rows_d[0:NE, :], rows_d[NE:2 * NE, :]
        gfin = glu_work
        ysum = xh
        logit_parts = over(kpad, 640, TT, P)
        tab = over(gates, 0, EXTRA, (PASSES - 1) * NE)
        tab2 = over(gates, 1536, EXTRA, (PASSES - 1) * NE)
        rel = over(kpad, 0, PASSES - 1, NE)
        pos, blockno, eids, zero96, enum = (over(kpad, 96, 96), over(kpad, 192, EXTRA), over(kpad, 208, EXTRA),
                                            over(kpad, 224, 96), over(kpad, 320, NE))

        bank = [ctx.enter_context(nc.psum_tensor(f"bank{i}", [P, 512], f32)) for i in range(8)]
        Y = [[bank[2 * t + h] for h in range(2)] for t in range(TT)]
        A, B, G, DN = bank[4], bank[5], bank[6], bank[7]
        ROUTER_BANKS = ((0, 1), (2, 7))

        x_loaded = [sem(f"x_loaded{t}") for t in range(TT)]
        vecs_loaded, small_loaded, k_swapped = sem("vecs_loaded"), sem("small_loaded"), sem("k_swapped")
        bgu_loaded, bdown_loaded, gfin_loaded, out_stored = sem("bgu_loaded"), sem("bdown_loaded"), sem("gfin_loaded"), sem("out_stored")
        moe_full = [sem(f"moe_full{i}") for i in range(MSLOTS)]
        further_full = [sem(f"further_full{i}") for i in range(MPE)]
        slot_full = [sem(f"slot_full{i}") for i in range(SLOTS)]
        piece_done = sem("piece_done")
        consts = sem("consts")
        u_zero, u_ready = sem("u_zero"), sem("u_ready")
        squares, squares_dve, stds = sem("squares"), sem("squares_dve"), sem("stds")
        z_out, gates_on = sem("z_out"), sem("gates_on")
        ln_sq, ln_std, ln_sig = sem("ln_sq"), sem("ln_std"), sem("ln_sig")
        exps, pt_out, ot_out = sem("exps"), sem("pt_out"), sem("ot_out")
        vecsT, cwT, xTp = sem("vecsT"), sem("cwT"), sem("xTp")
        vtr, s_done, pt_done, pv_done, ln_mean, ln_var = (sem("vtr"), sem("s_done"), sem("pt_done"), sem("pv_done"),
                                                          sem("ln_mean"), sem("ln_var"))
        hfT_done, logit_done, rank_done = sem("hfT_done"), sem("logit_done"), sem("rank_done")
        dve = sem("dve_step")
        vecs_out, cw_out, xh_ready, hT_ready, v_out = sem("vecs_out"), sem("cw_out"), sem("xh_ready"), sem("hT_ready"), sem("v_out")
        taps = sem("taps")
        s_masked, p_ready = sem("s_masked"), sem("p_ready")
        ln_cen, ln_z, silu_ready, sums_ready = sem("ln_cen"), sem("ln_z"), sem("silu_ready"), sem("sums_ready")
        residual_done, k_zeroed = sem("residual_done"), sem("k_zeroed")
        mean_out, ident4_ready, parts_done, parts_out = sem("mean_out"), sem("ident4_ready"), sem("parts_done"), sem("parts_out")
        logits_out, x_added, bdown_used = sem("logits_out"), sem("x_added"), sem("bdown_used")
        y_out, mixed_ready, xnew_ready = sem("y_out"), sem("mixed_ready"), sem("xnew_ready")
        hfT_ready, le_ready, member_ready, weights_ready, wT_out = (sem("hfT_ready"), sem("le_ready"), sem("member_ready"),
                                                                sem("weights_ready"), sem("wT_out"))
        le_exp, rstd_ready, cnt_out = sem("le_exp"), sem("rstd_ready"), sem("cnt_out")
        n_ready, ov_ready, ov_step = sem("n_ready"), sem("ov_ready"), sem("ov_step")
        sel_ready, gathered, xg_out, xT_done, xT_ready = sem("sel_ready"), sem("gathered"), sem("xg_out"), sem("xT_done"), sem("xT_ready")
        selw_ready, swT_done, swT_out = sem("selw_ready"), sem("swT_done"), sem("swT_out")
        gmin_ready, sig_ready, act_steps, act_ready = sem("gmin_ready"), sem("sig_ready"), sem("act_steps"), sem("act_ready")
        actT_done, actT_out, yb_out = sem("actT_done"), sem("actT_out"), sem("yb_out")
        y_done, gain_on, ysum_ready, ysum_ready2 = sem("y_done"), sem("gain_on"), sem("ysum_ready"), sem("ysum_ready2")

        def vec(name, c, rows=slice(0, P)):
            return vecs[rows, VEC[name][0] + c:VEC[name][0] + c + 1]

        def by_cols(n):
            return ring[:, n % SLOTS, :].rearrange("p (c n) -> p c n", c=C)

        def by_rows(n):
            return ring[:, n % SLOTS, :].rearrange("p (k n) -> p k n", k=KPP)

        def arrived(eng, n, later=0):
            eng.wait_ge(slot_full[n % SLOTS], 16 * (n // SLOTS + 1) + 16 * later)

        def moe_slot(m):
            s = m % MSLOTS
            if s < SLOTS:
                return by_rows(FRONT + s)
            return more[s - SLOTS].rearrange("p (k n) -> p k n", k=KPP)

        def blocks(eng, run):
            for r in range(CYCLE):
                run(r, r, 0)
            with eng.Fori(1, NE // CYCLE) as cycle:
                for r in range(CYCLE):
                    run(cycle * CYCLE + r, r, cycle)
            for r in range(NE % CYCLE):
                run(NE // CYCLE * CYCLE + r, r, NE // CYCLE)

        block = ctx.enter_context(nc.Block())

        @block.sync
        def _(sp):
            for t in range(TT):
                sp.dma_start(x[:, t, :], t_in["x"][0, t * P:(t + 1) * P, :]).then_inc(x_loaded[t], 16)
            for name, (row, n) in VEC.items():
                sp.dma_start(vrows[row:row + n, :], t_in[name].rearrange("(c p) -> c p", p=P)).then_inc(vecs_loaded, 16)
            sp.dma_start(cwrows, t_in["conv_w"]).then_inc(vecs_loaded, 16)

            def fetch(n, dst, src):
                if n >= SLOTS:
                    sp.wait_ge(piece_done, n - SLOTS + 1)
                sp.dma_start(dst, src).then_inc(slot_full[n % SLOTS], 16)

            w_in = t_in["w_in"].rearrange("(c p) n -> p c n", p=P)
            for n, col in enumerate(IN_COLS):
                fetch(n, by_cols(n), w_in[:, :, col:col + COLS])
            for first, name in ((CONV0, "w_conv_out"), (ATTN0, "w_attn_out")):
                w = t_in[name].rearrange("(c p) n -> p c n", p=P)
                for i in range(NO):
                    fetch(first + i, by_cols(first + i), w[:, :, COLS * i:COLS * (i + 1)])
            w = t_in["w_out"].rearrange("(i k p) n -> i p k n", p=P, k=KPP)
            for i in range(NW):
                fetch(WOUT0 + i, by_rows(WOUT0 + i), w[i])

            def piece_of(e, j):
                w = t_in[("w_gate", "w_up", "w_down")[j // NW]].rearrange("e (i k p) n -> e i p k n", p=P, k=KPP)
                if isinstance(e, int):
                    return w[e, j % NW]
                return w[bass.ds(e, 1), j % NW].rearrange("a p k n -> p (a k) n")

            def load(m, e, j):
                sp.dma_start(moe_slot(m), piece_of(e, j)).then_inc(moe_full[m % MSLOTS], 16)

            def first_piece(m, free, value):
                sp.wait_ge(free, value)
                load(m, m // MPE, m % MPE)

            load(SLOTS, SLOTS // MPE, SLOTS % MPE)
            first_piece(SLOTS + 1, piece_done, NZ)
            first_piece(SLOTS + 2, silu_ready, 1)
            first_piece(0, piece_done, FRONT - SLOTS + 1)
            first_piece(SLOTS + 3, pt_done, 12)
            first_piece(SLOTS + 4, pv_done, 4)
            for m in range(1, 8):
                first_piece(m, piece_done, FRONT + m - SLOTS + 1)
            first_piece(SLOTS + 5, piece_done, ATTN0 + NO)
            for m in range(8, SLOTS):
                first_piece(m, piece_done, FRONT + m - SLOTS + 1)
            first_piece(SLOTS + 6, piece_done, FRONT)
            sp.wait_ge(xh_ready, 2 * TT)
            first_piece(SLOTS + 7, x_added, 1)

            def expert_pieces(b, r, cycle):
                for j in range(MPE):
                    if isinstance(b, int) and b * MPE + j < MSLOTS:
                        continue
                    sp.wait_ge(piece_done, b * MPE + (FRONT + j - MSLOTS + 1))
                    load(r * MPE + j, b, j)

            blocks(sp, expert_pieces)
            sp.wait_ge(n_ready, 1)
            n_blocks = sp.value_load(nblk_i[0:1, 0:1], min_val=NE, max_val=NBLK)
            with sp.If(NE < n_blocks):
                sp.wait_ge(ov_ready, 1)
                sp.wait_ge(piece_done, FRONT + NE * MPE)
                with sp.Fori(NE, NBLK) as b:
                    with sp.If(b < n_blocks):
                        e = sp.value_load(eid_i[0:1, bass.ds(b - NE, 1)], min_val=0, max_val=NE - 1)
                        for j in range(MPE):
                            sp.wait_ge(piece_done, b * MPE + (FRONT + j - MPE + 1))
                            sp.dma_start(moe_slot(j), piece_of(e, j)).then_inc(further_full[j], 16)
            for t in range(TT):
                for h, half_ready in enumerate((ysum_ready, ysum_ready2)):
                    sp.wait_ge(half_ready, t + 1)
                    sp.dma_start(out[0, t * P:(t + 1) * P, h * 512:(h + 1) * 512],
                                 ysum[:, t, h * 512:(h + 1) * 512]).then_inc(out_stored, 16)
            sp.wait_ge(out_stored, 16 * 2 * TT)

        @block.gpsimd
        def _(pool):
            own = [0]

            def step(ins):
                own[0] += 1
                ins.then_inc(consts, 1)
                pool.wait_ge(consts, own[0])

            step(pool.memset(ident[:], 0.0))
            step(pool.affine_select(out=ident[:], in_=ident[:], compare_op=ALU.not_equal, fill=1.0, base=0,
                                    pattern=[[-1, P]], channel_multiplier=1))
            step(pool.memset(eps[:], EPS))
            assert own[0] == 3
            pool.memset(u[:, :, 0:KTAPS - 1], 0.0).then_inc(u_zero, 1)
            pool.memset(kpad[:], 0.0).then_inc(k_zeroed, 1)
            pool.dma_start(sinks[:], t_in["attn_sinks"].partition_broadcast(P)).then_inc(small_loaded, 16)
            pool.dma_start(brt[:], t_in["b_router"].partition_broadcast(P)).then_inc(small_loaded, 16)
            pool.dma_start(wrt[:], t_in["w_router"].rearrange("(c p) e -> p c e", p=P)).then_inc(small_loaded, 16)
            step(pool.memset(ones[:], 1.0))
            step(pool.memset(ones_h[:], 1.0))
            step(pool.memset(before[:], 1.0))
            step(pool.affine_select(out=before[:], in_=before[:], compare_op=ALU.is_gt, fill=0.0, base=0,
                                    pattern=[[1, P]], channel_multiplier=-1))
            step(pool.iota(ndist[:], pattern=[[1, 2 * P]], base=-P, channel_multiplier=-1,
                           allow_small_or_imprecise_dtypes=True))
            step(pool.affine_select(out=ndist[:], in_=ndist[:], compare_op=ALU.is_ge, fill=NEG, base=P,
                                    pattern=[[-1, 2 * P]], channel_multiplier=1))
            step(pool.affine_select(out=ndist[:], in_=ndist[:], compare_op=ALU.is_ge, fill=NEG, base=-1,
                                    pattern=[[1, 2 * P]], channel_multiplier=-1))
            step(pool.iota(iota[:], pattern=[[0, 2], [1, CAP]], base=1, channel_multiplier=0,
                           allow_small_or_imprecise_dtypes=True))
            for rows in (slice(0, NE), slice(NE, 2 * NE)):
                step(pool.iota(epart[rows, :], pattern=[[0, 1]], base=0, channel_multiplier=1,
                               allow_small_or_imprecise_dtypes=True))
            step(pool.memset(rank[:], 0.0))
            step(pool.memset(wts[:], 0.0))
            step(pool.memset(ehot[:], 0.0))
            for rows in (slice(0, NE), slice(NE, 2 * NE)):
                step(pool.affine_select(out=ehot[rows, 0:NE], in_=ehot[rows, 0:NE], compare_op=ALU.not_equal, fill=1.0,
                                        base=0, pattern=[[-1, NE]], channel_multiplier=1))
            pool.wait_ge(u_zero, 1)
            for i in range(N_GLUP // 2):
                pool.wait_ge(z_out, 2 * i + 2)
                pool.tensor_tensor(u[:, 2 * i:2 * i + 2, KTAPS - 1:], u[:, 2 * i:2 * i + 2, KTAPS - 1:],
                                   sigb[:, i % 2], ALU.mult).then_inc(u_ready, 1)
            pool.wait_ge(cwT, 1)
            pool.dma_start(bgate, t_in["b_gate"]).then_inc(bgu_loaded, 16)
            pool.dma_start(bup, t_in["b_up"]).then_inc(bgu_loaded, 16)
            pool.wait_ge(silu_ready, 1)
            pool.dma_start(bdown[0:NE, :], t_in["b_down"]).then_inc(bdown_loaded, 16)
            pool.wait_ge(bdown_used, 1)
            pool.dma_start(gfin, t_in["g_final"].partition_broadcast(P)).then_inc(gfin_loaded, 16)

        @block.scalar
        def _(act):
            act.wait_ge(consts, 3)
            act.preload_act_table(ACT.Sqrt)
            for t in range(TT):
                act.wait_ge(x_loaded[t], 16)
                act.activation(xh[:, t, :], x[:, t, :], ACT.Square, accum_out=ss[:, 0, t:t + 1]).then_inc(squares, 1)
                act.wait_ge(squares, t + 1)
                act.activation(std[:, 0, t:t + 1], ss[:, 0, t:t + 1], ACT.Sqrt, scale=1.0 / D, bias=eps[:, 0:1]).then_inc(stds, 1)

            act.wait_ge(vecs_out, 1)

            def evacuate(n, dst, func=ACT.Identity):
                act.wait_ge(piece_done, n + 1)
                for j in range(2):
                    last = act.activation(dst[j], bank[n % 3][:, j * T:(j + 1) * T], func,
                                          bias=vec("b_in", IN_COLS[n] // P + j))
                return last.then_inc(z_out, 1)

            for i in range(N_GLUP // 2):
                evacuate(2 * i, [u[:, 2 * i + j, KTAPS - 1:] for j in range(2)])
                if i >= 2:
                    act.wait_ge(u_ready, i - 1)
                act.wait_ge(piece_done, 2 * i + 2)
                for j in range(2):
                    last = act.activation(sigb[:, i % 2, j, :], bank[(2 * i + 1) % 3][:, j * T:(j + 1) * T], ACT.Sigmoid,
                                          bias=vec("b_in", IN_COLS[2 * i + 1] // P + j))
                last.then_inc(z_out, 1)
            for i in range(N_QP):
                evacuate(N_GLUP + i, [qT[:, 2 * i + j, :] for j in range(2)])
            act.wait_ge(k_zeroed, 1)
            act.wait_ge(piece_done, KV_PIECE + 1)
            for g in range(2):
                rows = slice(g * HD, (g + 1) * HD)
                act.activation(kpad[rows, 3 * g, :], bank[KV_PIECE % 3][rows, 0:T], ACT.Identity,
                               bias=vec("b_in", IN_COLS[KV_PIECE] // P, rows))
            act.activation(vT[:], bank[KV_PIECE % 3][:, T:2 * T], ACT.Identity,
                           bias=vec("b_in", IN_COLS[KV_PIECE] // P + 1)).then_inc(z_out, 1)
            act.wait_ge(z_out, KV_PIECE + 1)
            for g in range(2):
                act.dma_start(kpad[(1 - g) * HD:(2 - g) * HD, g + 1, :], kpad[g * HD:(g + 1) * HD, 3 * g, :]).then_inc(k_swapped, 16)

            def gate_piece(i):
                evacuate(GATE0 + i, [gates[:, 2 * i + j, :] for j in range(2)])

            def transposed_probs(q):
                if q >= 1:
                    act.wait_ge(pv_done, q)
                for k in range(3):
                    act.wait_ge(pt_done, 3 * q + k + 1)
                    act.activation(pt[:, k, :], bank[6 + k % 2][:], ACT.Copy).then_inc(pt_out, 1)

            def attention_out(q):
                act.wait_ge(pv_done, q + 1)
                for n in range(TT):
                    last = act.activation(oT[:, 2 * q:2 * q + 2, n * P:(n + 1) * P],
                                          bank[6 + n][:, 0:T].rearrange("p (c s) -> p c s", c=2), ACT.Copy)
                last.then_inc(ot_out, 1)

            def exponentials(q):
                act.wait_ge(s_masked, q + 1)
                for j in range(4):
                    for n, (lo, hi) in enumerate(((0, P), (P, 3 * P))):
                        act.activation(sc[:, q % 2, j, lo:hi], sc[:, q % 2, j, lo:hi], ACT.Exp, scale=SCALE,
                                       bias=sneg[:, q % 2, n, j:j + 1], accum_out=ssum[:, q % 2, n, j:j + 1])
                act.activation(ssnk[:, q % 2], ssnk[:, q % 2], ACT.Exp).then_inc(exps, 1)

            for i in range(4):
                gate_piece(i)
            exponentials(0)
            gate_piece(4)
            transposed_probs(0)
            act.wait_ge(ln_cen, 1)
            act.wait_ge(u_ready, N_GLUP // 2)
            act.activation(sq, cen[:], ACT.Square).then_inc(ln_sq, 1)
            exponentials(1)
            gate_piece(5)
            attention_out(0)
            transposed_probs(1)
            exponentials(2)
            gate_piece(6)
            act.wait_ge(ln_var, 1)
            act.activation(ln_stds, bank[3][:, 0:T], ACT.Sqrt, scale=1.0 / D, bias=eps[:, 0:1]).then_inc(ln_std, 1)
            attention_out(1)
            transposed_probs(2)
            act.wait_ge(ln_z, 1)
            act.activation(sq, cen[:], ACT.Sigmoid).then_inc(ln_sig, 1)
            gate_piece(7)
            attention_out(2)
            act.wait_ge(z_out, NZ)
            act.activation(gates[:], gates[:], ACT.Sigmoid).then_inc(gates_on, 1)
            exponentials(3)
            transposed_probs(3)
            attention_out(3)

            act.preload_act_table(ACT.Sqrt)
            for t in range(TT):
                act.wait_ge(xnew_ready, t + 1)
                act.activation(xh[:, t, :], x[:, t, :], ACT.Square, accum_out=ss[:, 1, t:t + 1]).then_inc(squares, 1)
            act.wait_ge(squares, 2 * TT)
            act.activation(std[:, 1, :], ss[:, 1, :], ACT.Sqrt, scale=1.0 / D, bias=eps[:, 0:1]).then_inc(stds, 1)
            act.preload_act_table(ACT.Exp)
            act.wait_ge(rstd_ready, 1)
            for t in range(TT):
                act.activation(xh[:, t, :], x[:, t, :], ACT.Copy, scale=rstd[:, 1, t:t + 1]).then_inc(xh_ready, 1)
            act.wait_ge(le_ready, 1)
            act.activation(rt[:, 4], rt[:, 4], ACT.Exp).then_inc(le_exp, 1)

            def copy_xg(k):
                act.wait_ge(gathered, k + 1)
                act.activation(xg, G[:], ACT.Copy).then_inc(xg_out, 1)

            def moe_block(b, then_gather=True):
                act.wait_ge(gmin_ready, b + 1)
                act.activation(sig, gmin, ACT.Sigmoid, scale=ALPHA).then_inc(sig_ready, 1)
                if then_gather:
                    act.wait_ge(act_steps, 2 * b + 1)
                    copy_xg(b + 1)
                act.wait_ge(actT_done, b + 1)
                act.activation(actT, A[:].rearrange("p (k h s) -> p k h s", k=4, h=2), ACT.Copy).then_inc(actT_out, 1)
                act.wait_ge(swT_done, b + 2)
                act.activation(swT, B[:, 0:T].rearrange("p (t s) -> p t s", t=TT), ACT.Copy).then_inc(swT_out, 1)
                act.wait_ge(piece_done, b * MPE + (FRONT + 3 * NW))
                act.activation(yb, DN[:], ACT.Copy).then_inc(yb_out, 1)

            copy_xg(0)
            with act.Fori(0, NE - 1) as b:
                moe_block(b)
            moe_block(NE - 1, then_gather=False)
            act.wait_ge(n_ready, 1)
            n_blocks = act.value_load(nblk_i[0:1, 0:1], min_val=NE, max_val=NBLK)
            with act.If(NE < n_blocks):
                copy_xg(NE)
                with act.Fori(NE, NBLK) as b:
                    with act.If(b < n_blocks):
                        moe_block(b)
            def half_scaled(t):
                act.wait_ge(rstd_ready, 2 + t)
                act.wait_ge(gain_on, 2 * t + 1)
                act.activation(ysum[:, t, 512:], ysum[:, t, 512:], ACT.Copy, scale=rstd[:, 0, t:t + 1]).then_inc(ysum_ready2, 1)

            act.preload_act_table(ACT.Sqrt)
            for t in range(TT):
                act.wait_ge(y_done, t + 1)
                for h in range(2):
                    if h == 1:
                        act.wait_ge(gain_on, 2 * t + 1)
                    act.activation((gmin, hidden)[h], Y[t][h][:], ACT.Square, accum_out=ss[:, 2 + h, t:t + 1]).then_inc(squares, 1)
                if t == TT - 1:
                    half_scaled(t - 1)
                act.wait_ge(squares_dve, 1 + t)
                act.activation(std[:, 0, t:t + 1], ss[:, 2, t:t + 1], ACT.Sqrt, scale=1.0 / D,
                               bias=eps[:, 0:1]).then_inc(stds, 1)
            half_scaled(TT - 1)

        @block.vector
        def _(dv):
            own = [0]

            def step(ins):
                own[0] += 1
                ins.then_inc(dve, 1)
                dv.wait_ge(dve, own[0])

            def normed_x(t):
                dv.wait_ge(stds, t + 1)
                step(dv.reciprocal(rstd[:, 0, t:t + 1], std[:, 0, t:t + 1]))
                dv.tensor_scalar(xh[:, t, :], x[:, t, :], rstd[:, 0, t:t + 1], None, ALU.mult).then_inc(xh_ready, 1)

            normed_x(0)
            normed_x(1)
            dv.wait_ge(vecsT, 1)
            dv.tensor_copy(vecs[:], bank[6][:, 0:VROWS]).then_inc(vecs_out, 1)
            dv.wait_ge(vecs_out, 1)
            g0 = VEC["g_mix"][0]
            for t in range(TT):
                for i in range(2):
                    dv.wait_ge(xTp, 2 * t + i + 1)
                    dv.tensor_tensor(hT[:, 4 * i:4 * i + 4, t * P:(t + 1) * P],
                                     bank[2 * t + i][:].rearrange("p (c s) -> p c s", c=4),
                                     vecs[:, g0 + 4 * i:g0 + 4 * i + 4].unsqueeze(2).to_broadcast([P, 4, P]),
                                     ALU.mult).then_inc(hT_ready, 1)
            dv.wait_ge(consts, 2)
            dv.reduce_sum(ident4[:], ident[:].rearrange("p (g e) -> p e g", e=NE), axis=X).then_inc(ident4_ready, 1)

            cb = VEC["conv_b"][0]
            dv.wait_ge(cwT, 1)
            dv.tensor_copy(cw, bank[7][:, 0:C * KTAPS].rearrange("p (c k) -> p c k", c=C)).then_inc(cw_out, 1)
            dv.wait_ge(small_loaded, 48)
            step(dv.tensor_scalar(sinks8[:], sinks[:], 1.0 / SCALE, None, ALU.mult))
            dv.wait_ge(cw_out, 1)
            with dv.Fori(0, C // 2) as i:
                dv.wait_ge(u_ready, i + 1)
                for k in range(KTAPS):
                    for j in range(2):
                        src = u[:, bass.ds(2 * i + j, 1), k:k + T].rearrange("p a t -> p (a t)")
                        dst = cv[:, bass.ds(2 * i + j, 1), :].rearrange("p a t -> p (a t)")
                        w = cw[:, bass.ds(2 * i + j, 1), k:k + 1].rearrange("p a t -> p (a t)")
                        if k == 0:
                            ins = dv.tensor_scalar(dst, src, w, vecs[:, bass.ds(cb + 2 * i + j, 1)], ALU.mult, ALU.add)
                        else:
                            dv.wait_ge(taps, 2 * KTAPS * i + 2 * k + j - 1)
                            ins = dv.scalar_tensor_tensor(dst, src, w, dst, ALU.mult, ALU.add)
                        ins.then_inc(taps, 1)
            dv.wait_ge(taps, C * KTAPS)

            def mask_and_max(q):
                heads = slice(4 * q, 4 * q + 4)
                dv.wait_ge(s_done, q + 1)
                if q == 0:
                    dv.wait_ge(consts, 10)
                if q >= 2:
                    dv.wait_ge(pt_done, 3 * (q - 1))
                for j in range(4):
                    slope = SLOPES[4 * q + j] / SCALE
                    dv.scalar_tensor_tensor(sc[:, q % 2, j, 0:P], ndist[:, P:2 * P], slope,
                                            bank[3][:, j * P:(j + 1) * P], ALU.mult, ALU.add)
                    last = dv.scalar_tensor_tensor(sc[:, q % 2, j, P:3 * P], ndist[:], slope,
                                                   bank[4 + j // 2][:, (j % 2) * T:(j % 2 + 1) * T], ALU.mult, ALU.add)
                step(last)
                dv.reduce_max(smax[:, 0, :], sc[:, q % 2, :, 0:P], axis=X)
                step(dv.reduce_max(smax[:, 1, :], sc[:, q % 2, :, P:3 * P], axis=X))
                snk = sinks8[:, heads].unsqueeze(1).to_broadcast([P, 2, 4])
                step(dv.tensor_tensor(smax[:], smax[:], snk, ALU.max))
                step(dv.tensor_scalar(sneg[:, q % 2], smax[:], -SCALE, None, ALU.mult))
                snk = sinks[:, heads].unsqueeze(1).to_broadcast([P, 2, 4])
                dv.tensor_tensor(ssnk[:, q % 2], sneg[:, q % 2], snk, ALU.add).then_inc(s_masked, 1)

            def divide(q):
                dv.wait_ge(exps, q + 1)
                step(dv.tensor_tensor(ssum[:, q % 2], ssum[:, q % 2], ssnk[:, q % 2], ALU.add))
                step(dv.reciprocal(ssum[:, q % 2], ssum[:, q % 2]))
                for n, (lo, hi) in enumerate(((0, P), (P, 3 * P))):
                    last = dv.tensor_tensor(sc[:, q % 2, :, lo:hi], sc[:, q % 2, :, lo:hi],
                                            ssum[:, q % 2, n, :].unsqueeze(2).to_broadcast([P, 4, hi - lo]), ALU.mult)
                last.then_inc(p_ready, 1)

            def out_piece(k, i):
                n = (CONV0, ATTN0)[k] + i
                dv.wait_ge(piece_done, n + 1)
                dv.wait_ge(gates_on, 1)
                for j in range(2):
                    c = 2 * i + j
                    last = dv.scalar_tensor_tensor(gates[:, k * C + c, :], bank[n % 3][:, j * T:(j + 1) * T],
                                                   vec(("b_conv_out", "b_attn_out")[k], c), gates[:, k * C + c, :],
                                                   ALU.add, ALU.mult)
                last.then_inc(y_out, 1)

            def further_blocks():
                NP = PASSES - 1
                own = [0]

                def step(ins):
                    own[0] += 1
                    ins.then_inc(ov_step, 1)
                    dv.wait_ge(ov_step, own[0])

                dv.wait_ge(yb_out, NE)
                dv.memset(zero96, 0.0)
                for i in range(EXTRA):
                    dv.memset(blockno[:, i:i + 1], float(i + 1))
                for e in range(NE):
                    last = dv.memset(enum[:, e:e + 1], float(e))
                step(last)
                ff = flag.rearrange("p a b -> p (a b)")
                step(dv.tensor_tensor_scan(pos, ff, zero96, 0.0, ALU.add, ALU.add))
                step(dv.tensor_tensor(tab, pos.unsqueeze(1).to_broadcast([P, EXTRA, NP * NE]),
                                      blockno.unsqueeze(2).to_broadcast([P, EXTRA, NP * NE]), ALU.is_equal))
                step(dv.tensor_tensor(tab, tab, ff.unsqueeze(1).to_broadcast([P, EXTRA, NP * NE]), ALU.mult))

                def picked(dst, values):
                    step(dv.tensor_tensor(tab2, tab, values.unsqueeze(1).to_broadcast([P, EXTRA, NP * NE]), ALU.mult))
                    step(dv.reduce_sum(dst, tab2, axis=X))

                relf = rel.rearrange("p a b -> p (a b)")
                for t in range(TT):
                    for k in range(NP):
                        last = dv.tensor_scalar(rel[:, k, :], rank[:, t, 0:NE], -float(CAP * (k + 1)), None, ALU.add)
                    step(last)
                    picked(rank[:, t, NE:NBLK], relf)
                    for k in range(NP):
                        last = dv.tensor_copy(rel[:, k, :], wts[:, t, 0:NE])
                    step(last)
                    picked(wts[:, t, NE:NBLK], relf)
                for k in range(NP):
                    last = dv.tensor_copy(rel[:, k, :], enum)
                step(last)
                picked(eids, relf)
                step(dv.tensor_scalar(ehot[:, NE:NBLK], eids[0:2 * NE, :], epart[:, 0:1], None, ALU.is_equal))
                dv.tensor_copy(eid_i[:], eids).then_inc(ov_ready, 1)

            dv.wait_ge(vtr, 1)
            dv.tensor_copy(v[:], bank[6][:, 0:T].rearrange("p (t c) -> p t c", t=TT)).then_inc(v_out, 1)
            mask_and_max(0)
            dv.reduce_sum(ln_sums, cv[:].rearrange("p c t -> p t c"), axis=X).then_inc(sums_ready, 1)
            divide(0)
            dv.wait_ge(ln_mean, 1)
            dv.tensor_scalar(ln_means, bank[3][:, 0:T], 1.0 / D, None, ALU.mult).then_inc(mean_out, 1)
            dv.wait_ge(mean_out, 1)
            dv.tensor_tensor(cen[:], cv[:], ln_means.unsqueeze(1).to_broadcast([P, C, T]), ALU.subtract).then_inc(ln_cen, 1)
            mask_and_max(1)
            dv.wait_ge(ln_sq, 1)
            dv.reduce_sum(ln_sums, sq.rearrange("p c t -> p t c"), axis=X).then_inc(sums_ready, 1)
            divide(1)
            mask_and_max(2)
            divide(2)
            dv.wait_ge(ln_std, 1)
            step(dv.reciprocal(ln_rstds, ln_stds))
            step(dv.tensor_tensor(cen[:], cen[:], ln_rstds.unsqueeze(1).to_broadcast([P, C, T]), ALU.mult))
            for c in range(C):
                last = dv.tensor_scalar(cen[:, c, :], cen[:, c, :], vec("conv_ln_g", c), vec("conv_ln_b", c), ALU.mult, ALU.add)
            last.then_inc(ln_z, 1)
            dv.wait_ge(ln_sig, 1)
            dv.tensor_tensor(cen[:], cen[:], sq, ALU.mult).then_inc(silu_ready, 1)
            mask_and_max(3)
            out_piece(0, 0)
            divide(3)
            for i in range(1, NO):
                out_piece(0, i)
            for i in range(NO):
                out_piece(1, i)
                dv.wait_ge(y_out, NO + i + 1)
                dv.tensor_tensor(gates[:, 2 * i:2 * i + 2, :], gates[:, 2 * i:2 * i + 2, :],
                                 gates[:, C + 2 * i:C + 2 * i + 2, :], ALU.add).then_inc(mixed_ready, 1)

            g1 = VEC["g_ffn"][0]
            for t in range(TT):
                for h in range(2):
                    if t == 0 or h == 0:
                        dv.wait_ge(residual_done, t + 1)
                    else:
                        dv.wait_ge(piece_done, FRONT)
                    last = dv.tensor_tensor(x[:, t, h * 512:(h + 1) * 512], x[:, t, h * 512:(h + 1) * 512],
                                            bank[3 + 2 * t + h][:], ALU.add)
                last.then_inc(xnew_ready, 1)
                for i in range(2):
                    dv.wait_ge(hfT_done, 2 * t + i + 1)
                    dv.tensor_tensor(hfT[:, 4 * i:4 * i + 4, t * P:(t + 1) * P],
                                     bank[ROUTER_BANKS[t][i]][:].rearrange("p (c s) -> p c s", c=4),
                                     vecs[:, g1 + 4 * i:g1 + 4 * i + 4].unsqueeze(2).to_broadcast([P, 4, P]),
                                     ALU.mult).then_inc(hfT_ready, 1)
                dv.wait_ge(parts_done, t + 1)
                dv.tensor_copy(logit_parts[:, t, :], bank[3][:, t * P:(t + 1) * P]).then_inc(parts_out, 1)
            dv.wait_ge(stds, TT + 1)
            dv.reciprocal(rstd[:, 1, :], std[:, 1, :]).then_inc(rstd_ready, 1)
            dv.wait_ge(rstd_ready, 1)

            L, gt, eq, cum, le, tmp = logits, rt[:, 0], rt[:, 1], rt[:, 2], rt[:, 4], rt[:, 5]
            dv.wait_ge(logit_done, TT)
            for t in range(TT):
                last = dv.scalar_tensor_tensor(L[:, t, :], bank[3][:, T + t * NE:T + (t + 1) * NE], rstd[:, 1, t:t + 1],
                                               brt[:], ALU.mult, ALU.add)
            last.then_inc(logits_out, 1)
            dv.wait_ge(logits_out, 1)
            dv.max(m8[:, 0, :], L[:, 0, :])
            step(dv.max(m8[:, 1, :], L[:, 1, :]))
            dv.tensor_tensor(le, L, m8[:, :, 0:1].to_broadcast([P, TT, NE]), ALU.subtract).then_inc(le_ready, 1)
            fourth = m8[:, :, TOPK - 1:TOPK].to_broadcast([P, TT, NE])
            dv.tensor_tensor(eq, L, fourth, ALU.is_equal)
            step(dv.tensor_tensor(gt, L, fourth, ALU.is_gt))
            for t in range(TT):
                step(dv.tensor_tensor_scan(cum[:, t, :], eq[:, t, :], eq[:, t, :], 0.0, ALU.add, ALU.max))
            step(dv.reduce_sum(quota[:, 0, :], gt, axis=X))
            step(dv.tensor_tensor(cum, cum, quota[:, 0, :].unsqueeze(2).to_broadcast([P, TT, NE]), ALU.add))
            step(dv.scalar_tensor_tensor(tmp, cum, float(TOPK), eq, ALU.is_le, ALU.mult))
            step(dv.tensor_tensor(member, gt, tmp, ALU.add))
            dv.tensor_copy(member_h[:], member).then_inc(member_ready, 1)
            dv.wait_ge(consts, 18)
            dv.wait_ge(rank_done, 1)
            step(dv.scalar_tensor_tensor(rank[:, :, 0:NE], bank[4][:, 0:TT * NE].rearrange("p (t e) -> p t e", t=TT), 1.0,
                                         member, ALU.add, ALU.mult))

            def select(b):
                if not isinstance(b, int) or b > 0:
                    dv.wait_ge(gathered, b)
                for t in range(TT):
                    last = dv.tensor_scalar(sel[:, t, :], iota[:, 0, :], rank[:, t, bass.ds(b, 1)], None, ALU.is_equal)
                last.then_inc(sel_ready, 1)

            def tokensT(b):
                dv.wait_ge(xT_done, b + 1)
                dv.tensor_scalar(bsel[0:2 * NE, :], ones[0:2 * NE, 0:CAP], ehot[:, bass.ds(b, 1)], None, ALU.mult)
                ge = vecs[:, g1:g1 + C].rearrange("p (h k) -> p k h", h=2).unsqueeze(3).to_broadcast([P, 4, 2, CAP])
                dv.tensor_tensor(xT, G[:].rearrange("p (k h s) -> p k h s", k=4, h=2), ge, ALU.mult).then_inc(xT_ready, 1)

            def moe_block(b, then_gather=True):
                if then_gather:
                    select(b + 1)
                dv.wait_ge(swT_done, b + 1)
                for t in range(TT):
                    last = dv.tensor_scalar(selw[:, t, :], iota[:].rearrange("p a s -> p (a s)"), rank[:, t, bass.ds(b, 1)],
                                            wts[:, t, bass.ds(b, 1)], ALU.is_equal, ALU.mult)
                last.then_inc(selw_ready, 1)
                dv.wait_ge(piece_done, b * MPE + (FRONT + NW))
                dv.tensor_scalar(gmin, A[:], LIMIT, None, ALU.min).then_inc(gmin_ready, 1)
                dv.wait_ge(sig_ready, b + 1)
                dv.tensor_tensor(gmin, gmin, sig, ALU.mult).then_inc(act_steps, 1)
                dv.wait_ge(piece_done, b * MPE + (FRONT + 2 * NW))
                dv.tensor_scalar(uclip, B[:], LIMIT, -LIMIT, ALU.min, ALU.max).then_inc(act_steps, 1)
                dv.wait_ge(act_steps, 2 * b + 2)
                dv.scalar_tensor_tensor(hidden, uclip, 1.0, gmin, ALU.add, ALU.mult).then_inc(act_ready, 1)
                if then_gather:
                    tokensT(b + 1)

            select(0)
            dv.tensor_copy(cnt, bank[4][:, TT * NE:(TT + 1) * NE]).then_inc(cnt_out, 1)
            dv.wait_ge(le_exp, 1)
            step(dv.tensor_tensor(le, le, member, ALU.mult))
            step(dv.reduce_sum(quota[:, 1, :], le, axis=X))
            step(dv.reciprocal(quota[:, 2, :], quota[:, 1, :]))
            dv.tensor_tensor(wts[:, :, 0:NE], le, quota[:, 2, :].unsqueeze(2).to_broadcast([P, TT, NE]),
                             ALU.mult).then_inc(weights_ready, 1)
            dv.wait_ge(cnt_out, 1)
            for k in range(1, PASSES):
                last = dv.tensor_scalar(flag[:, k - 1, :], cnt, float(CAP * k), None, ALU.is_gt)
            step(last)
            step(dv.reduce_sum(nblk_f[:, 0:1], flag.rearrange("p a b -> p (a b)"), axis=X))
            dv.tensor_scalar(nblk_i[:], nblk_f[:, 0:1], float(NE), None, ALU.add).then_inc(n_ready, 1)
            tokensT(0)
            dv.wait_ge(swT_done, 1)
            dv.tensor_copy(wT, bank[5][0:NE, 0:T]).then_inc(wT_out, 1)
            with dv.Fori(0, NE - 1) as b:
                moe_block(b)
            moe_block(NE - 1, then_gather=False)

            n_blocks = dv.value_load(nblk_i[0:1, 0:1], min_val=NE, max_val=NBLK)
            with dv.If(NE < n_blocks):
                further_blocks()
                select(NE)
                tokensT(NE)
                with dv.Fori(NE, NBLK) as b:
                    with dv.If(b < n_blocks):
                        moe_block(b)

            dv.wait_ge(gfin_loaded, 16)
            for t in range(TT):
                dv.wait_ge(y_done, t + 1)
                for h in (1, 0):
                    if h == 0:
                        dv.wait_ge(squares, 2 * TT + 2 * t + 1)
                    cols = slice(h * 512, (h + 1) * 512)
                    dv.tensor_tensor(ysum[:, t, cols], Y[t][h][:], gfin[:, cols], ALU.mult).then_inc(gain_on, 1)
                dv.wait_ge(squares, 2 * TT + 2 * t + 2)
                dv.tensor_tensor(ss[:, 2, t:t + 1], ss[:, 2, t:t + 1], ss[:, 3, t:t + 1], ALU.add).then_inc(squares_dve, 1)
                dv.wait_ge(stds, TT + 2 + t)
                dv.reciprocal(rstd[:, 0, t:t + 1], std[:, 0, t:t + 1]).then_inc(rstd_ready, 1)
                dv.wait_ge(rstd_ready, 2 + t)
                dv.wait_ge(gain_on, 2 * t + 2)
                dv.tensor_scalar(ysum[:, t, 0:512], ysum[:, t, 0:512], rstd[:, 0, t:t + 1], None, ALU.mult).then_inc(ysum_ready, 1)

        @block.tensor
        def _(pe):
            pe.wait_ge(consts, 2)

            def to_columns(src, t, banks, ready, done):
                pe.wait_ge(ready, t + 1)
                for i in range(2):
                    for j in range(4):
                        c = 4 * i + j
                        last = pe.transpose(bank[banks[i]][:, j * P:(j + 1) * P], src[:, t, c * P:(c + 1) * P], ident[:])
                    last.then_inc(done, 1)

            to_columns(xh, 0, (0, 1), xh_ready, xTp)
            pe.wait_ge(vecs_loaded, 16 * (len(VEC) + 1))
            pe.transpose(bank[6][:, 0:VROWS], vrows, ident[0:VROWS, 0:VROWS]).then_inc(vecsT, 1)
            to_columns(xh, 1, (2, 3), xh_ready, xTp)
            for c in range(C):
                last = pe.transpose(bank[7][:, c * KTAPS:(c + 1) * KTAPS], cwrows[:, c * P:(c + 1) * P],
                                    ident[0:KTAPS, 0:KTAPS])
            last.then_inc(cwT, 1)
            pe.wait_ge(hT_ready, 4)

            def project(n, src):
                arrived(pe, n)
                if n >= 3:
                    m = n - 3
                    if m < NZ:
                        pe.wait_ge(z_out, m + 1)
                    else:
                        pe.wait_ge(y_out, m - NZ + 1)
                w = by_cols(n)
                for j in range(2):
                    for c in range(C):
                        last = pe.matmul(bank[n % 3][:, j * T:(j + 1) * T], w[:, c, j * P:(j + 1) * P], src[:, c, :],
                                         start=(c == 0), stop=(c == C - 1))
                last.then_inc(piece_done, 1)

            def scores(q):
                if q == 0:
                    pe.wait_ge(k_swapped, 32)
                else:
                    pe.wait_ge(s_masked, q)
                for n in (1, 0):
                    keys = slice(0, (n + 1) * P)
                    if n == 0 and q == 1:
                        pe.wait_ge(mean_out, 1)
                    if n == 0 and q == 3:
                        pe.wait_ge(ln_std, 1)
                    for j in range(2):
                        dst = bank[3][:, j * T:(j + 1) * T] if n == 0 else bank[4 + j][:]
                        last = pe.matmul(dst, qT[:, 2 * q + j, n * P:(n + 1) * P],
                                         kpad[:, q // 2 * 2:q // 2 * 2 + 2, keys], start=True, stop=True)
                last.then_inc(s_done, 1)

            def turn_probs(q):
                pe.wait_ge(p_ready, q + 1)
                if q >= 1:
                    pe.wait_ge(ot_out, q)
                for k in range(3):
                    if k == 2:
                        pe.wait_ge(pt_out, 3 * q + 1)
                    for j in range(4):
                        last = pe.transpose(bank[6 + k % 2][:, j * P:(j + 1) * P],
                                            sc[:, q % 2, j, k * P:(k + 1) * P], ident[:])
                    last.then_inc(pt_done, 1)

            def attend(q):
                pe.wait_ge(pt_out, 3 * q + 3)
                kv = slice(q // 2 * HD, (q // 2 + 1) * HD)
                for dst, keys, k, start, stop in ((6, 0, 0, True, True), (7, 0, 1, True, False), (7, 1, 2, False, True)):
                    for par in range(2):
                        probs = pt[:, k, :].rearrange("p (c two s) -> p c two s", c=2, two=2)[:, :, par, :]
                        last = pe.matmul(bank[dst][par * HD:(par + 1) * HD, 0:T], v[:, keys, kv], probs,
                                         start=start, stop=stop)
                last.then_inc(pv_done, 1)

            def sum_over_partitions(k, masked, done):
                pe.wait_ge(sums_ready, k + 1)
                pe.wait_ge(s_masked, masked)
                pe.matmul(bank[3][:, 0:T], ones[:], ln_sums, start=True, stop=True).then_inc(done, 1)

            for n in range(GATE0 + 1):
                project(n, hT)
            pe.wait_ge(z_out, GATE0)
            pe.wait_ge(vecs_out, 1)
            for t in range(TT):
                last = pe.transpose(bank[6][:, t * P:(t + 1) * P], vT[:, t * P:(t + 1) * P], ident[:])
            last.then_inc(vtr, 1)
            scores(0)
            for i in range(1, 5):
                project(GATE0 + i, hT)
            sum_over_partitions(0, 1, ln_mean)
            scores(1)
            pe.wait_ge(cw_out, 1)
            pe.wait_ge(v_out, 1)
            turn_probs(0)
            project(GATE0 + 5, hT)
            attend(0)
            scores(2)
            turn_probs(1)
            project(GATE0 + 6, hT)
            sum_over_partitions(1, 3, ln_var)
            attend(1)
            scores(3)
            turn_probs(2)
            project(GATE0 + 7, hT)
            attend(2)
            pe.wait_ge(silu_ready, 1)
            project(CONV0, cen)
            project(CONV0 + 1, cen)
            turn_probs(3)
            project(CONV0 + 2, cen)
            attend(3)
            project(CONV0 + 3, cen)
            pe.wait_ge(ot_out, 4)
            for i in range(NO):
                project(ATTN0 + i, oT)

            def residual(t, i):
                arrived(pe, WOUT0 + i)
                pe.wait_ge(mixed_ready, i + 1)
                for h in range(2):
                    for k in range(KPP):
                        last = pe.matmul(bank[3 + 2 * t + h][:], gates[:, 2 * i + k, t * P:(t + 1) * P],
                                         by_rows(WOUT0 + i)[:, k, h * 512:(h + 1) * 512],
                                         start=(i == 0 and k == 0), stop=(i == NW - 1 and k == KPP - 1))
                    if t == 1 and h == 0 and i == NW - 1:
                        last.then_inc(residual_done, 1)
                return last

            def router_logits(t):
                pe.wait_ge(hfT_ready, 2 * t + 2)
                for c in range(C):
                    rows = slice(c % 4 * NE, (c % 4 + 1) * NE)
                    last = pe.matmul(bank[3][rows, t * P:(t + 1) * P], wrt[:, c, :], hfT[:, c, t * P:(t + 1) * P],
                                     start=(c < 4), stop=(c >= 4))
                last.then_inc(parts_done, 1)

            def sum_of_parts(t):
                pe.wait_ge(parts_out, t + 1)
                pe.wait_ge(ident4_ready, 1)
                pe.matmul(bank[3][:, T + t * NE:T + (t + 1) * NE], logit_parts[:, t, :], ident4[:],
                          start=True, stop=True).then_inc(logit_done, 1)

            def add_x(t, h):
                return pe.matmul(Y[t][h][:], ident[:], x[:, t, h * 512:(h + 1) * 512], start=True, stop=False)

            for i in range(NW):
                last = residual(0, i)
            last.then_inc(residual_done, 1)
            for i in range(NW):
                last = residual(1, i)
                last.then_inc(piece_done, 1)
                if i == 1:
                    to_columns(x, 0, ROUTER_BANKS[0], xnew_ready, hfT_done)
                if i == 2:
                    router_logits(0)
            sum_of_parts(0)
            to_columns(x, 1, ROUTER_BANKS[1], xnew_ready, hfT_done)
            router_logits(1)
            sum_of_parts(1)
            for t, h in ((0, 0), (0, 1), (1, 0)):
                add_x(t, h)
            pe.wait_ge(logits_out, 1)
            add_x(1, 1).then_inc(x_added, 1)
            pe.wait_ge(member_ready, 1)
            pe.matmul(bank[4][:, 0:NE], before[:], member_h[:, 0, :], start=True, stop=True)
            pe.matmul(bank[4][:, NE:2 * NE], ones_h[:], member_h[:, 0, :], start=True, stop=False)
            pe.matmul(bank[4][:, NE:2 * NE], before[:], member_h[:, 1, :], start=False, stop=True)
            pe.matmul(bank[4][:, 2 * NE:3 * NE], ones_h[:], member_h[:, 0, :], start=True, stop=False)
            pe.matmul(bank[4][:, 2 * NE:3 * NE], ones_h[:], member_h[:, 1, :], start=False, stop=True).then_inc(rank_done, 1)

            def gather(k):
                pe.wait_ge(sel_ready, k + 1)
                for t in range(TT):
                    for h in range(2):
                        last = pe.matmul(G[h * CAP:(h + 1) * CAP, :], sel[:, t, :], xh[:, t, h * 512:(h + 1) * 512],
                                         start=(t == 0), stop=(t == TT - 1))
                last.then_inc(gathered, 1)

            def tokensT(k):
                pe.wait_ge(xg_out, k + 1)
                for i in range(4):
                    last = pe.transpose(G[:, i * P:(i + 1) * P], xg[:, i * P:(i + 1) * P], ident[:])
                last.then_inc(xT_done, 1)

            def scatter(ends=False):
                for t in range(TT):
                    for h in range(2):
                        rows = slice(h * CAP, (h + 1) * CAP)
                        last = pe.matmul(Y[t][h][:], swT[rows, t, :], yb[rows, :], start=False, stop=ends)
                    if ends:
                        last.then_inc(y_done, 1)

            def product(dst, first, piece, lhs, bias):
                for i in range(NW):
                    j = first + i
                    w = piece(j)
                    for k in range(KPP):
                        for h in range(2):
                            last = pe.matmul(dst[h * CAP:(h + 1) * CAP, :], lhs(KPP * i + k), w[:, k, h * 512:(h + 1) * 512],
                                             start=(i == 0 and k == 0), stop=(i == NW - 1 and k == KPP - 1))
                    last.then_inc(piece_done, 1)
                    if i == 0 and bias is not None:
                        rows = slice(0, NE) if bias is bgate else slice(NE, 2 * NE)
                        for h in range(2):
                            pe.matmul(dst[h * CAP:(h + 1) * CAP, :], bsel[rows, :], bias[:, h * 512:(h + 1) * 512],
                                      start=False, stop=False)

            def start_y():
                pe.wait_ge(wT_out, 1)
                pe.wait_ge(bdown_loaded, 16)
                for t in range(TT):
                    for h in range(2):
                        last = pe.matmul(Y[t][h][:], wT[:, t * P:(t + 1) * P], bdown[0:NE, h * 512:(h + 1) * 512],
                                         start=False, stop=False)
                last.then_inc(bdown_used, 1)

            def piece_of_cycle(r, cycle):
                def piece(j):
                    m = r * MPE + j
                    pe.wait_ge(moe_full[m % MSLOTS], cycle * (16 * CYCLE * MPE // MSLOTS) + 16 * (m // MSLOTS + 1))
                    return moe_slot(m)
                return piece

            def piece_of_further(i):
                def piece(j):
                    pe.wait_ge(further_full[j], i * 16 + 16)
                    return moe_slot(j)
                return piece

            def moe_block(b, piece):
                first = isinstance(b, int) and b == 0
                then_gather = not (isinstance(b, int) and b == NE - 1)
                pe.wait_ge(xT_ready, b + 1)
                product(A, 0, piece, lambda c: xT[:, c % 4, c // 4, :], bgate)
                if first:
                    pe.wait_ge(wT_out, 1)
                else:
                    pe.wait_ge(swT_out, b)
                if not first:
                    pe.wait_ge(yb_out, b)
                    scatter()
                product(B, NW, piece, lambda c: xT[:, c % 4, c // 4, :], bup)
                if then_gather:
                    gather(b + 1)
                if first:
                    start_y()
                pe.wait_ge(act_ready, b + 1)
                for i in range(4):
                    last = pe.transpose(A[:, i * P:(i + 1) * P], hidden[:, i * P:(i + 1) * P], ident[:])
                last.then_inc(actT_done, 1)
                if then_gather:
                    tokensT(b + 1)
                pe.wait_ge(selw_ready, b + 1)
                for t in range(TT):
                    last = pe.transpose(B[:, t * P:(t + 1) * P], selw[:, t, :], ident[:])
                last.then_inc(swT_done, 1)
                pe.wait_ge(actT_out, b + 1)
                product(DN, 2 * NW, piece, lambda c: actT[:, c % 4, c // 4, :], None)

            pe.wait_ge(xh_ready, 2 * TT)
            gather(0)
            tokensT(0)
            pe.wait_ge(weights_ready, 1)
            for t in range(TT):
                last = pe.transpose(bank[5][0:NE, t * P:(t + 1) * P], wts[:, t, 0:NE], ident[:])
            last.then_inc(swT_done, 1)
            pe.wait_ge(bgu_loaded, 32)
            blocks(pe, lambda b, r, cycle: moe_block(b, piece_of_cycle(r, cycle)))
            pe.wait_ge(n_ready, 1)
            n_blocks = pe.value_load(nblk_i[0:1, 0:1], min_val=NE, max_val=NBLK)
            with pe.If(NE < n_blocks):
                gather(NE)
                tokensT(NE)
                with pe.Fori(NE, NBLK) as b:
                    with pe.If(b < n_blocks):
                        moe_block(b, piece_of_further(b - NE))
            pe.wait_ge(yb_out, n_blocks)
            pe.wait_ge(swT_out, n_blocks)
            scatter(True)



_ORDER = ["x", "g_mix", "w_in", "b_in", "conv_w", "conv_b", "conv_ln_g", "conv_ln_b", "w_conv_out", "b_conv_out",
          "attn_sinks", "w_attn_out", "b_attn_out", "w_out", "g_ffn", "w_router", "b_router", "w_gate", "b_gate",
          "w_up", "b_up", "w_down", "b_down", "g_final"]


def kernel(**inputs):
    import numpy as np
    import concourse.bacc as bacc
    from concourse.bass_utils import run_bass_kernel_spmd

    nc = bacc.Bacc("TRN2", target_bir_lowering=False, num_devices=1)
    arrays, aps = {}, {}
    for name in _ORDER:
        a = np.ascontiguousarray(inputs[name])
        arrays[f"in_{name}"] = a
        aps[name] = nc.dram_tensor(f"in_{name}", a.shape, mybir.dt.from_np(a.dtype), kind="ExternalInput").ap()
    out = nc.dram_tensor("out_y", (1, T, D), mybir.dt.float32, kind="ExternalOutput").ap()
    build(nc, aps, out)
    r = run_bass_kernel_spmd(nc, [arrays], core_ids=[0])
    return r.results[0]["out_y"]
```
